# Optimizing a Trainium2 kernel written in Bass

```python
import jax, jax.numpy as jnp
from jax import lax
import numpy as np

D_MODEL = 2048
BATCH = 1
SEQ = 256
DEPTH = 2

CHUNK = 64
N_A_LAYERS = DEPTH // 2
N_B_LAYERS = DEPTH - N_A_LAYERS
RWKV_HEAD_SIZE = 64
RWKV_HEADS = D_MODEL // RWKV_HEAD_SIZE
DECAY_LORA = max(32, int(round(D_MODEL ** 0.5 * 1.8 / 32)) * 32)
AAA_LORA = max(32, int(round(D_MODEL ** 0.5 * 1.8 / 32)) * 32)
GATE_LORA = max(32, int(round(D_MODEL ** 0.8 * 0.6 / 32)) * 32)
GN_EPS = 64e-5
HEAD_DIM = 64
N_Q_HEADS = D_MODEL // HEAD_DIM
GQA_GROUP = 8
N_KV_HEADS = N_Q_HEADS // GQA_GROUP
WINDOW = 128
WINDOW_CHUNKS = WINDOW // CHUNK
ATTN_SCALE = HEAD_DIM ** -0.5
NEG_INF = -1e30
ROT_DIM = HEAD_DIM // 4
ROPE_THETA = 500000.0
D_FF = ((8 * D_MODEL // 3 + 255) // 256) * 256
RMS_EPS = 1e-6

kernel_name = "yoco_rwkv7_swa_sink_hybrid"

def rms_norm(x, g):
    xf = x.astype(jnp.float32)
    y = xf * lax.rsqrt(jnp.mean(xf * xf, axis=-1, keepdims=True) + RMS_EPS)
    return (y * g.astype(jnp.float32)).astype(x.dtype)

def modulate(h, shift, scale):
    return h * (1 + scale[:, None, :]) + shift[:, None, :]

def rope_partial(x, positions):
    inv_freq = ROPE_THETA ** (-jnp.arange(0, ROT_DIM, 2, dtype=jnp.float32) / ROT_DIM)
    ang = positions.astype(jnp.float32)[..., None] * inv_freq
    cos, sin = jnp.cos(ang)[:, :, None, :], jnp.sin(ang)[:, :, None, :]
    xr = x[..., :ROT_DIM].astype(jnp.float32)
    x1, x2 = xr[..., :ROT_DIM // 2], xr[..., ROT_DIM // 2:]
    rot = jnp.concatenate([x1 * cos - x2 * sin, x2 * cos + x1 * sin], axis=-1)
    return jnp.concatenate([rot.astype(x.dtype), x[..., ROT_DIM:]], axis=-1)

def wkv7_scan(r, decay, k, v, kk, a):
    B, T, H, N = r.shape

    def step(S, inp):
        r_t, w_t, k_t, v_t, kk_t, a_t = inp
        sa = jnp.einsum('bhvk,bhk->bhv', S, -kk_t)
        S = (S * w_t[:, :, None, :]
             + sa[..., None] * (kk_t * a_t)[:, :, None, :]
             + v_t[..., None] * k_t[:, :, None, :])
        return S, jnp.einsum('bhvk,bhk->bhv', S, r_t)

    S0 = jnp.zeros((B, H, N, N), jnp.float32)
    seq = tuple(jnp.moveaxis(t, 1, 0) for t in (r, decay, k, v, kk, a))
    _, y = lax.scan(step, S0, seq)
    return jnp.moveaxis(y, 0, 1)

def rwkv7_time_mix(h, mu, w_r, w_k, w_v, w0, w1, w2, a0, a1, a2, g1, g2,
                   k_k, k_a, r_k, gn_g, gn_b, w_o):
    B, T, D = h.shape
    H, N = RWKV_HEADS, RWKV_HEAD_SIZE
    xx = jnp.pad(h, ((0, 0), (1, 0), (0, 0)))[:, :-1] - h
    mix = lambda i: h + xx * mu[i]
    r = mix(0) @ w_r
    w_log = -jax.nn.softplus(-(w0 + jnp.tanh(mix(1) @ w1) @ w2)) - 0.5
    k = mix(2) @ w_k
    v = mix(3) @ w_v
    a = jax.nn.sigmoid(a0 + (mix(4) @ a1) @ a2)
    g = jax.nn.sigmoid(mix(5) @ g1) @ g2
    heads = lambda t: t.reshape(B, T, H, N).astype(jnp.float32)
    kk = heads(k * k_k)
    kk = kk / jnp.maximum(jnp.sqrt(jnp.sum(kk * kk, axis=-1, keepdims=True)), 1e-12)
    k = k * (1 + (a - 1) * k_a)
    decay = jnp.exp(-jnp.exp(heads(w_log)))
    rh, kh, vh = heads(r), heads(k), heads(v)
    y = wkv7_scan(rh, decay, kh, vh, kk, heads(a))
    mean = jnp.mean(y, axis=-1, keepdims=True)
    var = jnp.mean(jnp.square(y - mean), axis=-1, keepdims=True)
    y = ((y - mean) * lax.rsqrt(var + GN_EPS) * gn_g.reshape(H, N).astype(jnp.float32)
         + gn_b.reshape(H, N).astype(jnp.float32))
    y = y + jnp.sum(rh * kh * r_k.astype(jnp.float32), axis=-1, keepdims=True) * vh
    y = y.reshape(B, T, D).astype(h.dtype)
    return (y * g) @ w_o

def band_keys(t):
    nC = t.shape[1]
    parts = [jnp.pad(t, ((0, 0), (s, 0), (0, 0), (0, 0), (0, 0)))[:, :nC]
             for s in range(WINDOW_CHUNKS - 1, -1, -1)]
    return jnp.concatenate(parts, axis=2)

def swa_sink_attention(q, k, v, sinks):
    B, T = q.shape[0], q.shape[1]
    nC = T // CHUNK
    qc = q.reshape(B, nC, CHUNK, N_KV_HEADS, GQA_GROUP, HEAD_DIM)
    kb = band_keys(k.reshape(B, nC, CHUNK, N_KV_HEADS, HEAD_DIM))
    vb = band_keys(v.reshape(B, nC, CHUNK, N_KV_HEADS, HEAD_DIM))
    key_shift = WINDOW_CHUNKS - 1 - jnp.arange(WINDOW_CHUNKS * CHUNK) // CHUNK
    valid = jnp.arange(nC)[:, None] >= key_shift[None, :]
    s = jnp.einsum('bnqhgd,bnkhd->bhgnqk', qc, kb).astype(jnp.float32) * ATTN_SCALE
    s = jnp.where(valid[None, None, None, :, None, :], s, NEG_INF)
    sink = sinks.astype(jnp.float32).reshape(N_KV_HEADS, GQA_GROUP)[None, :, :, None, None, None]
    m = jnp.maximum(jnp.max(s, axis=-1, keepdims=True), sink)
    p = jnp.exp(s - m)
    p = p / (jnp.sum(p, axis=-1, keepdims=True) + jnp.exp(sink - m))
    o = jnp.einsum('bhgnqk,bnkhd->bnqhgd', p.astype(v.dtype), vb)
    return o.reshape(B, T, N_Q_HEADS * HEAD_DIM)

def swiglu(h, w_gu, w_down):
    gate, up = jnp.split(h @ w_gu, 2, axis=-1)
    return (jax.nn.silu(gate) * up) @ w_down

def setup_inputs(seed: int = 0) -> dict:
    key = jax.random.key(seed)
    ks = iter(jax.random.split(key, 40))
    nrm = lambda shape, s: jax.random.normal(next(ks), shape, jnp.float32) * s
    D, NA, NB, H, N = D_MODEL, N_A_LAYERS, N_B_LAYERS, RWKV_HEADS, RWKV_HEAD_SIZE
    KVW = N_KV_HEADS * HEAD_DIM
    QW = N_Q_HEADS * HEAD_DIM
    x = nrm((BATCH, SEQ, D), 1.0)
    c = nrm((BATCH, D), 1.0)
    offset = jax.random.randint(next(ks), (BATCH, 1), 0, 64, dtype=jnp.int32) * CHUNK
    positions = (offset + jnp.arange(SEQ, dtype=jnp.int32)[None, :]).astype(jnp.int32)
    return {
        "x": x,
        "c": c,
        "positions": positions,
        "ada_w": nrm((DEPTH, D, 6 * D), 0.5 * D ** -0.5),
        "ada_b": nrm((DEPTH, 6 * D), 0.02),
        "norm_g": 1.0 + nrm((DEPTH, 4, D), 0.05),
        "rwkv_mu": jax.random.uniform(next(ks), (NA, 6, D), jnp.float32),
        "rwkv_w_r": nrm((NA, D, D), D ** -0.5),
        "rwkv_w_k": nrm((NA, D, D), D ** -0.5),
        "rwkv_w_v": nrm((NA, D, D), D ** -0.5),
        "rwkv_w0": jax.random.uniform(next(ks), (NA, D), jnp.float32, -6.0, 1.0),
        "rwkv_w1": nrm((NA, D, DECAY_LORA), D ** -0.5),
        "rwkv_w2": nrm((NA, DECAY_LORA, D), 0.5 * DECAY_LORA ** -0.5),
        "rwkv_a0": nrm((NA, D), 0.1),
        "rwkv_a1": nrm((NA, D, AAA_LORA), D ** -0.5),
        "rwkv_a2": nrm((NA, AAA_LORA, D), AAA_LORA ** -0.5),
        "rwkv_g1": nrm((NA, D, GATE_LORA), D ** -0.5),
        "rwkv_g2": nrm((NA, GATE_LORA, D), GATE_LORA ** -0.5),
        "rwkv_k_k": 0.85 + nrm((NA, D), 0.05),
        "rwkv_k_a": 1.0 + nrm((NA, D), 0.05),
        "rwkv_r_k": nrm((NA, H, N), 0.1),
        "rwkv_gn_g": 1.0 + nrm((NA, D), 0.05),
        "rwkv_gn_b": nrm((NA, D), 0.02),
        "rwkv_w_o": nrm((NA, D, D), D ** -0.5),
        "kv_ada_w": nrm((D, 2 * D), 0.5 * D ** -0.5),
        "kv_ada_b": nrm((2 * D,), 0.02),
        "kv_norm_g": 1.0 + nrm((D,), 0.05),
        "w_kv": nrm((D, 2 * KVW), D ** -0.5),
        "attn_w_q": nrm((NB, D, QW), D ** -0.5),
        "attn_sinks": nrm((NB, N_Q_HEADS), 1.0),
        "attn_w_o": nrm((NB, QW, D), QW ** -0.5),
        "ffn_w_gu": nrm((DEPTH, D, 2 * D_FF), D ** -0.5),
        "ffn_w_down": nrm((DEPTH, D_FF, D), D_FF ** -0.5),
    }

def reference(x, c, positions, ada_w, ada_b, norm_g,
              rwkv_mu, rwkv_w_r, rwkv_w_k, rwkv_w_v, rwkv_w0, rwkv_w1, rwkv_w2,
              rwkv_a0, rwkv_a1, rwkv_a2, rwkv_g1, rwkv_g2, rwkv_k_k, rwkv_k_a, rwkv_r_k,
              rwkv_gn_g, rwkv_gn_b, rwkv_w_o,
              kv_ada_w, kv_ada_b, kv_norm_g, w_kv,
              attn_w_q, attn_sinks, attn_w_o,
              ffn_w_gu, ffn_w_down):
    B, T, D = x.shape
    c_act = jax.nn.silu(c)
    k_sh = v_sh = None
    for layer in range(DEPTH):
        mods = c_act @ ada_w[layer] + ada_b[layer]
        sh_m, sc_m, g_m, sh_f, sc_f, g_f = jnp.split(mods, 6, axis=-1)
        h = modulate(rms_norm(x, norm_g[layer, 0]), sh_m, sc_m)
        if layer < N_A_LAYERS:
            i = layer
            y = rwkv7_time_mix(h, rwkv_mu[i], rwkv_w_r[i], rwkv_w_k[i], rwkv_w_v[i],
                               rwkv_w0[i], rwkv_w1[i], rwkv_w2[i], rwkv_a0[i], rwkv_a1[i],
                               rwkv_a2[i], rwkv_g1[i], rwkv_g2[i], rwkv_k_k[i], rwkv_k_a[i],
                               rwkv_r_k[i], rwkv_gn_g[i], rwkv_gn_b[i], rwkv_w_o[i])
        else:
            if layer == N_A_LAYERS:
                kv_shift, kv_scale = jnp.split(c_act @ kv_ada_w + kv_ada_b, 2, axis=-1)
                hk = modulate(rms_norm(x, kv_norm_g), kv_shift, kv_scale)
                k_sh, v_sh = jnp.split(hk @ w_kv, 2, axis=-1)
                k_sh = rope_partial(k_sh.reshape(B, T, N_KV_HEADS, HEAD_DIM), positions)
                v_sh = v_sh.reshape(B, T, N_KV_HEADS, HEAD_DIM)
            j = layer - N_A_LAYERS
            q = rope_partial((h @ attn_w_q[j]).reshape(B, T, N_Q_HEADS, HEAD_DIM), positions)
            y = swa_sink_attention(q, k_sh, v_sh, attn_sinks[j]) @ attn_w_o[j]
        x = x + g_m[:, None, :] * rms_norm(y, norm_g[layer, 1])
        h = modulate(rms_norm(x, norm_g[layer, 2]), sh_f, sc_f)
        x = x + g_f[:, None, :] * rms_norm(swiglu(h, ffn_w_gu[layer], ffn_w_down[layer]), norm_g[layer, 3])
    return x


_drawn_inputs = setup_inputs


def setup_inputs(seed=0):
    import zlib

    import numpy as np

    out = dict(_drawn_inputs(seed))
    spreads = {}
    factors = {'rwkv_w1': 4.741,
     'rwkv_w2': 4.646,
     'rwkv_a0': 4.638,
     'rwkv_k_k': 3.28,
     'rwkv_gn_g': 3.685,
     'rwkv_gn_b': 7.992,
     'kv_ada_b': 3.361,
     'kv_norm_g': 5.085,
     'attn_sinks': 8.0}
    for name, (base, spread) in spreads.items():
        noise = np.random.default_rng([zlib.crc32(name.encode()), seed]).standard_normal(out[name].shape)
        drawn = base * np.exp(spread * noise) if base else spread * noise
        out[name] = __import__('jax').numpy.asarray(drawn.astype(out[name].dtype))
    for name, factor in factors.items():
        out[name] = (out[name] * factor).astype(out[name].dtype)
    return out
```

```python
from contextlib import ExitStack

import numpy as np
import concourse.bass as bass
from concourse import mybir
from concourse.alu_op_type import AluOpType as ALU

F32 = mybir.dt.float32
F32R = mybir.dt.float32r
I32 = mybir.dt.int32
ACT = mybir.ActivationFunctionType
AX = mybir.AxisListType

P = 128
D = 2048
T = 256
KT = D // P
DFF = 5632
HT = DFF // P
C = 64
NC = T // C
LORA = 96
GLORA = 256
W_SCALE = float(np.exp(-0.5))
RMS_EPS = 1e-6
GN_EPS = 64e-5
ATT_SCALE = 64 ** -0.5
LEVELS = [2, 4, 8, 16, 32]
SCAN_LINKS = 16
ATT_LINKS = 6
UNITS = 28
U_KV, U_1 = 12, 16
TWO_PI_HI = 6.28125
TWO_PI_LO = float(np.float32(2 * np.pi - 6.28125))
MAGIC = 1.5 * 2.0 ** 23


def constants():
    parts, at, n = [], {}, 0

    def put(name, a):
        nonlocal n
        at[name] = (n, n + a.shape[1])
        n += a.shape[1]
        parts.append(np.asarray(a, np.float32))

    p = np.arange(P)
    e, s = p // 64, p % 64
    t = np.arange(64)
    put("ident", np.eye(P))
    put("head_ones", (e[:, None] == e[None, :]) * 1.0)
    put("stacked_ident", (s[:, None] == t[None, :]) * 1.0)
    rot = np.where(s < 8, p + 8, np.where(s < 16, p - 8, p))
    swap = np.zeros((P, P))
    swap[rot[s < 16], p[s < 16]] = 1.0
    put("rope_swap", swap)
    for half in range(2):
        put(f"dup{half}", (p[:, None] == (64 * half + s)[None, :]) * 1.0)
    bd = (e[:, None, None] == np.arange(2)[None, :, None])
    put("strict", (bd * (t[None, None, :] > s[:, None, None])).reshape(P, 128))
    put("incl", (bd * (t[None, None, :] >= s[:, None, None])).reshape(P, 128))
    low = lambda r, c, m: ((r // m) % 2 == 1) & (c // m == r // m - 1)
    put("upper1", low(t[None, :], s[:, None], 1) * 1.0)
    for m in [1] + LEVELS:
        put(f"lower{m}", low(s[:, None], t[None, :], m) * 1.0)
    put("carry", np.broadcast_to((np.arange(T) % C != 0) * 1.0, (P, T)))
    freq = np.float32(500000.0) ** (-np.arange(0, 16, 2, dtype=np.float32) / np.float32(16))
    put("freq", np.where(s < 16, freq[s % 8], 0.0)[:, None])
    put("rope_sign", np.where(s < 8, -1.0, np.where(s < 16, 1.0, 0.0))[:, None])
    put("rms_eps", np.full((P, 1), RMS_EPS))
    return np.ascontiguousarray(np.concatenate(parts, 1)), at


PARTS = [(8, 4), (8, 4), (6, 3)]


def plan():
    order = [("r", 4, 4), ("k", 4, 4), ("v", 4, 4), ("o", 4, 4)]
    for n, (g, q) in enumerate(PARTS):
        order += [(f"gu0{n}", g, 4), (f"down0{n}", 4, q)]
    order += [("kv", 1, 4), ("q", 4, 4), ("ao", 4, 4)]
    for n, (g, q) in enumerate(PARTS):
        order += [(f"gu1{n}", g, 4), (f"down1{n}", 4, q)]
    stages, panel, group = {}, 0, 12
    for name, g, q in order:
        stages[name] = dict(name=name, groups=g, q=q, p0=panel, g0=group)
        panel += g * q
        group += g
    return stages, panel


CARRY = {"gu00": 12, "gu01": 16, "gu02": 20, "kv": 23, "q": 24, "ao": 26}


def trunk(nc, a, at, out):
    stages, PANELS = plan()
    names = list(stages)

    def after(name):
        k = names.index(name) + 1
        return stages[names[k]] if k < len(names) else None

    ctx = ExitStack()
    base = 16512
    here = [base]

    def sb(name, shape, dt=F32, offset=None):
        size = int(np.prod(shape[1:])) * 4
        if offset is None:
            offset = here[0]
            here[0] += (size + 31) // 32 * 32
        return nc.alloc_sbuf_tensor_at(name, shape, dt, offset=offset)

    def sem(name):
        return ctx.enter_context(nc.semaphore(name))

    X = sb("X", [P, KT, T])
    MH = sb("MH", [P, KT, T], F32R)
    ML = sb("ML", [P, KT, T], F32R)
    RAW = [sb(f"RAW{n}", [P, 4, 512]) for n in range(4)]
    WH = [sb(f"WH{n}", [P, 4, 512], F32R) for n in range(2)]
    WL = [sb(f"WL{n}", [P, 4, 512], F32R) for n in range(2)]
    ADA = [sb(f"ADA{n}", [P, 1024]) for n in range(4)]
    ACC = sb("ACC", [P, 1024])
    ncst = max(b for _, b in at.values())
    CST = sb("CST", [P, ncst])
    PM = sb("PM", [P, 640])
    MODS = sb("MODS", [P, UNITS * 8])
    CA = sb("CA", [P, KT])
    ONES = sb("ONES", [P, P])
    ONESB = sb("ONESB", [P, P], mybir.dt.bfloat16)
    RS = sb("RS", [P, T])
    RT = sb("RT", [P, T])
    SV = sb("SV", [P, KT])
    GG = sb("GG", [P, KT])
    OMK = sb("OMK", [P, KT])
    arena = here[0]
    K = 1024
    H = sb("H", [P, KT, T], offset=arena)
    XX = sb("XX", [P, KT, T], offset=arena + 16 * K)
    MIX = sb("MIX", [P, KT, T], offset=arena + 32 * K)
    ST = [sb(f"ST{n}", [P, 4, T], offset=arena + (48 + 4 * n) * K) for n in range(2)]
    XIN = sb("XIN", [P, 2, D], offset=arena + 32 * K)
    PROW = sb("PROW", [P, 5, P], offset=arena + 48 * K)
    TW = sb("TW", [LORA, T], offset=arena + 56 * K)
    AW = sb("AW", [LORA, T], offset=arena + 57 * K)
    GW = sb("GW", [P, 2, T], offset=arena + 58 * K)
    Y = sb("Y", [P, KT, T], offset=arena)
    HH = sb("HH", [P, 16, T], F32R, offset=arena + 16 * K)
    HL = sb("HL", [P, 16, T], F32R, offset=arena + 32 * K)
    SQ = [sb(f"SQ{n}", [P, 4, T], offset=arena + (48 + 4 * n) * K) for n in range(2)]
    SG = [sb(f"SG{n}", [P, 2, T], offset=arena + (48 + 2 * n) * K) for n in range(2)]
    HID = [sb(f"HID{n}", [P, 2, T], offset=arena + (52 + 2 * n) * K) for n in range(2)]
    top = [arena]

    def sc(name, *shape):
        size = (int(np.prod(shape)) * 4 + 31) // 32 * 32
        top[0] += size
        return sb(name, [P, *shape], offset=top[0] - size)

    IN = [sc(f"IN{n}", 6, T) for n in range(2)]
    KKR, KSQ, KK, CUM, CME, WI, WV, WE, T1, KP, RR, KKA, BV = (sc(n, T) for n in (
        "KKR", "KSQ", "KK", "CUM", "CME", "WI", "WV", "WE", "T1", "KP", "RR", "KKA", "BV"))
    AR = sc("AR", NC, 2, C)
    BST = sc("BST", NC, C)
    BDAR = sc("BDAR", NC, 2, 2, C)
    BDB, BDK, BDV = sc("BDB", NC, 2, C), sc("BDK", NC, 2, C), sc("BDV", NC, 2, C)
    AST = sc("AST", NC, C)
    AM = [sc(f"AM{n}", NC, C) for n in range(2)]
    NT = sc("NT", NC, 2, C)
    PC = sc("PC", NC, C)
    NBD, ARB, AAK, ARK = (sc(n, NC, 2, C) for n in ("NBD", "ARB", "AAK", "ARK"))
    TOKV = sc("TOKV", NC, C)
    TOKBK = sc("TOKBK", 2, NC, C)
    SS, SW, RH, UU = sc("SS", C), sc("SW", C), sc("RH", C), sc("UU", C)
    YC, YQ = sc("YC", NC, C), sc("YQ", NC, C)
    YBD = sc("YBD", NC, 2, C)
    Y2 = sc("Y2", T)
    MS, VS, VR, HALF = sc("MS", NC), sc("VS", NC), sc("VR", NC), sc("HALF", NC)
    scan_top = top[0]
    top[0] = arena + 16 * K
    QR = Y
    KR, VR2, KX = sc("KR", 2, T), sc("VTR", 2, T), sc("KX", 2, T)
    KD, VW = sc("KD", 4, T), sc("VW", NC, T)
    QS = [sc(f"QS{n}", T) for n in range(2)]
    QT = [sc(f"QT{n}", T) for n in range(2)]
    PR = [sc(f"PR{n}", NC, P) for n in range(2)]
    PT = [sc(f"PT{n}", NC, P) for n in range(2)]
    COS, SIN, ANG, TURN = sc("COS", T), sc("SIN", T), sc("ANG", T), sc("TURN", T)
    assert top[0] <= arena + 48 * K
    top[0] = arena + 56 * K
    SNK, SNKA = sc("SNK", KT), sc("SNKA", 2 * KT)
    MX, NM, SU, ES, DEN = ([sc(f"{n}{m}", NC) for m in range(2)] for n in ("MX", "NM", "SU", "ES", "DEN"))
    POSI = sb("POSI", [P, T], I32, offset=arena + 57 * K)
    XO = sb("XO", [P, 2, D], offset=arena + 16 * K)
    assert scan_top <= 229344 and arena + 60 * K <= 229344, (scan_top, arena)

    PG = [nc.alloc_psum_tensor(f"PG{n}", [P, 1024], F32) for n in range(2)]
    PS = nc.alloc_psum_tensor("PS", [P, 512], F32)
    PA = nc.alloc_psum_tensor("PA", [P, 512], F32)
    PT0 = nc.alloc_psum_tensor("PT0", [P, 512], F32)
    PT1 = nc.alloc_psum_tensor("PT1", [P, 512], F32)
    PTT = [PT0, PT1]

    SCR = nc.dram_tensor("scan_inputs", [KT, P, 6, T], F32, kind="Internal").ap()

    cst = lambda name: CST[:, at[name][0]:at[name][1]]
    col = {}
    for l in range(2):
        for i in range(4):
            col[f"g{l}{i}"] = (4 * l + i) * 16
    col["bias"] = 128
    col["kvg"], col["c"] = 352, 368
    for i in range(6):
        col[f"mu{i}"] = 384 + 16 * i
    col["w0"], col["a0"] = 480, 496
    for n, name in enumerate(["k_k", "k_a", "r_k", "gn_g", "gn_b"]):
        col[name] = 512 + 16 * n
    pm = lambda name: PM[:, col[name]:col[name] + 16]
    MOD = {}
    for l, u in ((0, 0), (1, U_1)):
        for i, name in enumerate(["sh_m", "sc_m", "g_m", "sh_f", "sc_f", "g_f"]):
            MOD[f"{name}{l}"] = 8 * u + 16 * i
    MOD["sh_kv"], MOD["sc_kv"] = 8 * U_KV, 8 * U_KV + 16
    mod = lambda name: MODS[:, MOD[name]:MOD[name] + 16]

    cst_full, par_full, x_full = sem("cst_full"), sem("par_full"), sem("x_full")
    raw_full = [sem(f"raw_full{n}") for n in range(4)]
    lora_full = [sem(f"lora_full{n}") for n in range(4)]
    ada_full = [sem(f"ada_full{n}") for n in range(4)]
    in_full = [sem(f"in_full{n}") for n in range(2)]
    scr_stored = [sem(f"scr_stored{n}") for n in range(2)]
    out_stored, att_full = sem("out_stored"), sem("att_full")
    wh_ready, wl_ready, wlp_ready = sem("wh_ready"), sem("wl_ready"), sem("wlp_ready")
    panel_used = sem("panel_used")
    mh_ready, ml_ready = sem("mh_ready"), sem("ml_ready")
    hh_ready, hl_ready, sg_ready, hid_ready = sem("hh_ready"), sem("hl_ready"), sem("sg_ready"), sem("hid_ready")
    ada_used, red_done, mods_ready = sem("ada_used"), sem("red_done"), sem("mods_ready")
    ones_set, par_turned, par_copied, ca_ready = sem("ones_set"), sem("par_turned"), sem("par_copied"), sem("ca_ready")
    x_turned, x_copied = sem("x_turned"), sem("x_copied")
    squared, sq_used, rt_ready, rs_ready = sem("squared"), sem("sq_used"), sem("rt_ready"), sem("rs_ready")
    scaled, h_ready, mix_ready, mix_used, mix_full = sem("scaled"), sem("h_ready"), sem("mix_ready"), sem("mix_used"), sem("mix_full")
    lora_mid, lora_done = sem("lora_mid"), sem("lora_done")
    st_ready, y_ready, x_ready, v_step = sem("st_ready"), sem("y_ready"), sem("x_ready"), sem("v_step")
    (kkr_ready, ksq_ready, ss_done, nrm_ready, cum_ready, exp_ready, rr_ready, ar_ready, b_ready, bdk_ready,
     bd_ready, scores_done, tok_done, nt_ready, am_ready, coef_ready, ast_ready, tok_ready, p_done, p_copied,
     d_done, nbd_ready, rhs_done, rhs_ready, u_done, u_ready, sd_done, s_ready, y_done, yc_ready, yq_ready,
     vs_ready, vr_ready, ybd_ready, yt_done, yo_ready, bonus_used, zeroed, half_set) = (sem(n) for n in (
         "kkr_ready ksq_ready ss_done nrm_ready cum_ready exp_ready rr_ready ar_ready b_ready bdk_ready "
         "bd_ready scores_done tok_done nt_ready am_ready coef_ready ast_ready tok_ready p_done p_copied "
         "d_done nbd_ready rhs_done rhs_ready u_done u_ready sd_done s_ready y_done yc_ready yq_ready "
         "vs_ready vr_ready ybd_ready yt_done yo_ready bonus_used zeroed half_set").split())
    (kv_copied, q_copied, rope_ready, swap_done, roped, kd_done, kd_ready, vw_done, vw_ready, sco_done, max_ready,
     prob_ready, es_ready, norm_ready, pt_done, pt_ready, o_done, turned, drained, sin_ready) = (sem(n) for n in (
         "kv_copied q_copied rope_ready swap_done roped kd_done kd_ready vw_done vw_ready sco_done max_ready "
         "prob_ready es_ready norm_ready pt_done pt_ready o_done turned drained sin_ready").split())

    block = ctx.enter_context(nc.Block())

    class Tally:
        def __init__(self, semaphore, value=0):
            self.sem, self.v, self.k = semaphore, value, 0

        def add(self, ins):
            ins.then_inc(self.sem, 1)
            self.v, self.k = self.v + 1, self.k + 1
            return self.v

    gu = [a["ffn_w_gu"][l].rearrange("(k p) (h n) -> p k h n", p=P, h=2) for l in range(2)]
    down = [a["ffn_w_down"][l].rearrange("(k p) n -> p k n", p=P) for l in range(2)]
    square = {"r": a["rwkv_w_r"][0], "k": a["rwkv_w_k"][0], "v": a["rwkv_w_v"][0], "o": a["rwkv_w_o"][0],
              "kv": a["w_kv"], "q": a["attn_w_q"][0], "ao": a["attn_w_o"][0]}
    square = {n: w.rearrange("(k p) n -> p k n", p=P) for n, w in square.items()}

    def halves(st, g, q):
        name, slot = st["name"], (st["p0"] + (g * st["q"] if isinstance(g, int) else 0) + q) % 4
        raw = RAW[slot]
        if name.startswith("gu"):
            g_all = g + sum(x for x, _ in PARTS[:int(name[3])])
            w = gu[int(name[2])]
            return slot, [(raw[:, :, 256 * h:256 * h + 256], w[:, 4 * q:4 * q + 4, h, bass.ds(g_all * 256, 256)])
                          for h in range(2)]
        if name.startswith("down"):
            k0 = 16 * int(name[5]) + 4 * q
            w = down[int(name[4])]
        else:
            k0, w = 4 * q, square[name]
        return slot, [(raw[:, 2 * h:2 * h + 2, :], w[:, k0 + 2 * h:k0 + 2 * h + 2, bass.ds(g * 512, 512)])
                      for h in range(2)]

    ada = [a["ada_w"][l].rearrange("(k p) n -> k p n", p=P) for l in range(2)]
    kva = a["kv_ada_w"].rearrange("(k p) n -> k p n", p=P)

    def ada_source(first, u, step):
        w, c0 = (ada[0], 0) if first < U_KV else (kva, U_KV) if first < U_1 else (ada[1], U_1)
        return w[step][:, bass.ds((first - c0 + u) * 1024, 1024)]

    @block.sync
    def _(sp):
        def ada_load(first, u, step):
            n = 16 * (first + u) + step
            if not (isinstance(n, int) and n < 4):
                sp.wait_ge(ada_used, n - 3)
            sp.dma_start(ADA[step % 4][:, :], ada_source(first, u, step)).then_inc(ada_full[step % 4], 16)

        def panel_load(st, g, q):
            n = st["p0"] + g * st["q"] + q
            slot, parts = halves(st, g, q)
            if isinstance(n, int) and n < 4:
                sp.wait_ge(lora_done, [4, 8, 12, 12][n])
            else:
                sp.wait_ge(wl_ready, n - 3)
                sp.wait_ge(wlp_ready, n - 3)
            for dst, src in parts:
                sp.dma_start(dst, src).then_inc(raw_full[slot], 16)

        def stage_loads(st):
            name, n = st["name"], st["groups"]
            first = CARRY.get(name)
            nxt = after(name)

            def body(g, u, odd, target, tg):
                for q in range(4):
                    if first is not None:
                        for s in range(4 if name == "kv" else 2):
                            ada_load(first, u, (4 if name == "kv" else 2) * q + s + (8 if odd else 0))
                    if target is not None and q < target["q"]:
                        panel_load(target, tg, q)

            if n > 4:
                with sp.Fori(0, n // 2 - 1) as i:
                    body(2 * i, i, False, st, 2 * i + 1)
                    body(2 * i + 1, i, True, st, 2 * i + 2)
                body(n - 2, n // 2 - 1, False, st, n - 1)
            else:
                for g in range(n - 1):
                    body(g, g // 2, g % 2 == 1, st, g + 1)
            body(n - 1, (n - 1) // 2, n > 1, nxt, 0)

        sp.dma_start(CST[:, :], a["cst"]).then_inc(cst_full, 16)
        for u in range(2):
            for s in range(16):
                ada_load(u, 0, s)
        sp.dma_start(XIN[:, :, :], a["x"][0].rearrange("(h p) d -> p h d", p=P)).then_inc(x_full, 16)
        for u in range(2, 4):
            for s in range(16):
                ada_load(u, 0, s)
        lora_tile = lambda n, w: RAW[n][:, :, :].rearrange("p a b -> p (a b)")[:, 0:w]
        for n, name in enumerate(["rwkv_w1", "rwkv_a1"]):
            sp.dma_start(lora_tile(n, KT * LORA).rearrange("p (k n) -> p k n", k=KT),
                         a[name][0].rearrange("(k p) n -> p k n", p=P)).then_inc(lora_full[n], 16)
        g1 = a["rwkv_g1"][0].rearrange("(k p) n -> p k n", p=P)
        for n in range(2):
            sp.dma_start(RAW[2 + n][:, :, :].rearrange("p a (b n) -> p (a b) n", b=2),
                         g1[:, 8 * n:8 * n + 8, :]).then_inc(lora_full[2 + n], 16)
        for n, name in enumerate(["rwkv_w2", "rwkv_a2"]):
            sp.wait_ge(mix_used, KT * (n + 1))
            sp.dma_start(RAW[n][0:LORA, :, :].rearrange("p a b -> p (a b)"), a[name][0]).then_inc(lora_full[n], 16)
        sp.wait_ge(mix_used, 3 * KT)
        for n in range(2):
            sp.dma_start(RAW[2 + n][:, :, :].rearrange("p a b -> p (a b)"),
                         a["rwkv_g2"][0][P * n:P * n + P, :]).then_inc(lora_full[2 + n], 16)
        for q in range(4):
            panel_load(stages["r"], 0, q)
        for name in ("r", "k"):
            stage_loads(stages[name])
        for g in range(1, 4):
            for q in range(4):
                panel_load(stages["v"], g, q)
        for q in range(4):
            panel_load(stages["o"], 0, q)
        for stores in scr_stored:
            sp.wait_ge(stores, 16 * 12)
        for n in range(2):
            sp.dma_start(IN[n][:, :, :], SCR[n]).then_inc(in_full[n], 16)
        for s in range(4):
            ada_load(4, 0, s)
        with sp.Fori(0, 7) as i:
            for tt in range(2):
                for s in range(4):
                    ada_load(4, i, 8 * tt + 4 + s)
                sp.wait_ge(ml_ready, 12 + 2 * i + tt + 1)
                sp.dma_start(IN[tt][:, :, :], SCR[bass.ds(2 * i + tt + 2, 1)].rearrange("a p q t -> p (a q) t"))\
                  .then_inc(in_full[tt], 16)
                for s in range(4):
                    if tt == 0:
                        ada_load(4, i, 8 + s)
                    else:
                        ada_load(4, i + 1, s)
        for s in range(4, 16):
            ada_load(4, 7, s)
        for name in names[names.index("o"):]:
            if name == "q":
                sp.dma_start(SNKA[:, :], a["attn_sinks"].to_broadcast([P, 2 * KT])).then_inc(att_full, 16)
                sp.dma_start(POSI[:, :], a["positions"][0:1, :].to_broadcast([P, T])).then_inc(att_full, 16)
            stage_loads(stages[name])
        sp.wait_ge(drained, 8)
        sp.dma_start(out[0].rearrange("(h p) d -> p h d", p=P), XO[:, :, :]).then_inc(out_stored, 16)
        sp.wait_ge(out_stored, 16)

    @block.gpsimd
    def _(pool):
        def residue(n, q):
            pool.wait_ge(wh_ready, n + 1)
            if not (isinstance(n, int) and n < 2):
                pool.wait_ge(panel_used, n - 1)
            pool.tensor_tensor(WL[q % 2][:, 2:4, :], RAW[q][:, 2:4, :], WH[q % 2][:, 2:4, :].bitcast(F32),
                               ALU.subtract).then_inc(wlp_ready, 1)

        pool.memset(ONES[:, :], 1.0).then_inc(ones_set, 1)
        pool.memset(ONESB[:, :], 1.0).then_inc(ones_set, 1)
        for n in range(4):
            residue(n, n)
        with pool.Fori(1, 12) as i:
            for q in range(4):
                residue(4 * i + q, q)
        residue(48, 0)
        for stores in scr_stored:
            pool.wait_ge(stores, 16 * 12)
        pool.wait_ge(panel_used, 48)
        for z in (BDAR, BDB, BDK, BDV, NBD, YBD):
            flat = z[:, :, :, :, :].rearrange("p a b c d -> p (a b c d)") if z is BDAR else \
                z[:, :, :, :].rearrange("p a b c -> p (a b c)")
            pool.memset(flat, 0.0).then_inc(zeroed, 1)
        pool.memset(HALF[:, :], -0.5).then_inc(half_set, 1)
        pool.wait_ge(half_set, 1)
        with pool.Fori(0, KT) as n:
            pool.wait_ge(vs_ready, n + 1)
            pool.tensor_tensor(VR[:, :], VS[:, :], HALF[:, :], ALU.pow).then_inc(vr_ready, 1)
        for q in range(1, 4):
            residue(48 + q, q)
        with pool.Fori(13, PANELS // 4) as i:
            for q in range(4):
                residue(4 * i + q, q)

    @block.scalar
    def _(act):
        def rounded(n, slot=None, full=None):
            if isinstance(n, int):
                slot, full = n % 4, 32 * (n // 4) + 32
            act.wait_ge(raw_full[slot], full)
            if not (isinstance(n, int) and n < 2):
                act.wait_ge(panel_used, n - 1)
            act.activation(WH[slot % 2][:, :, :], RAW[slot][:, :, :], ACT.Copy).then_inc(wh_ready, 1)

        stored = [0]

        def to_scratch(gi, tiles, quantity, make, wait):
            k = stored[0]
            act.wait_ge(*wait)
            if k >= 2:
                act.wait_ge(scr_stored[k % 2], 16 * (k // 2))
            make(ST[k % 2], PG[gi % 2])
            act.wait_ge(st_ready, k + 1)
            act.dma_start(SCR[tiles:tiles + 4, :, quantity, :].rearrange("j p n -> p j n"), ST[k % 2][:, :, :])\
               .then_inc(scr_stored[k % 2], 16)
            stored[0] += 1

        def rooted(n):
            act.wait_ge(sq_used, 4 * n + 4)
            if n:
                act.wait_ge(rs_ready, n)
            act.activation(RT[:, :], PS[:, 0:T], ACT.Sqrt, bias=cst("rms_eps"), scale=1.0 / D).then_inc(rt_ready, 1)

        nsq = [0]

        def squares(src, ready):
            for q in range(4):
                act.wait_ge(*ready(q))
                if nsq[0] >= 2:
                    act.wait_ge(sq_used, nsq[0] - 1)
                act.activation(SQ[nsq[0] % 2][:, :, :], src[:, 4 * q:4 * q + 4, :], ACT.Square).then_inc(squared, 1)
                nsq[0] += 1

        def shifted(nh, shift, free):
            for k in range(KT):
                act.wait_ge(scaled, nh + k + 1)
                if k % 4 == 0 and free is not None:
                    act.wait_ge(panel_used, free + k // 4 + 1)
                act.activation(MH[:, k, :], Y[:, k, :], ACT.Identity, bias=mod(shift)[:, k:k + 1]).then_inc(mh_ready, 1)

        rows = [(0, 0, a["norm_g"].rearrange("l i (k n) -> (l i k) n", n=P)),
                (1, 0, a["ada_b"][0:1].rearrange("a (k n) -> (a k) n", n=P)),
                (1, 96, a["kv_ada_b"].rearrange("(k n) -> k n", n=P)),
                (2, 0, a["ada_b"][1:2].rearrange("a (k n) -> (a k) n", n=P)),
                (2, 96, a["kv_norm_g"].rearrange("(k n) -> k n", n=P)),
                (2, 112, a["c"].rearrange("a (k n) -> (a k) n", n=P)),
                (3, 0, a["rwkv_mu"][0].rearrange("i (k n) -> (i k) n", n=P)),
                (3, 96, a["rwkv_w0"].rearrange("a (k n) -> (a k) n", n=P)),
                (3, 112, a["rwkv_a0"].rearrange("a (k n) -> (a k) n", n=P)),
                (4, 0, a["rwkv_k_k"].rearrange("a (k n) -> (a k) n", n=P)),
                (4, 16, a["rwkv_k_a"].rearrange("a (k n) -> (a k) n", n=P)),
                (4, 32, a["rwkv_r_k"][0].rearrange("(k e) n -> k (e n)", e=2)),
                (4, 48, a["rwkv_gn_g"].rearrange("a (k n) -> (a k) n", n=P)),
                (4, 64, a["rwkv_gn_b"].rearrange("a (k n) -> (a k) n", n=P))]
        for b, r, src in rows:
            act.dma_start(PROW[r:r + src.shape[0], b, :], src).then_inc(par_full, 16)
        act.wait_ge(par_turned, 1)
        act.activation(PM[:, 0:592], PG[0][:, 0:592], ACT.Copy).then_inc(par_copied, 1)
        act.wait_ge(par_copied, 1)
        act.activation(CA[:, :], pm("c"), ACT.Silu).then_inc(ca_ready, 1)
        for g in range(4):
            act.wait_ge(x_turned, g + 1)
            act.activation(X[:, 4 * g:4 * g + 4, :], PG[g % 2][:, :].rearrange("p (j t) -> p j t", j=4),
                           ACT.Copy).then_inc(x_copied, 1)
        squares(X, lambda q: (x_copied, 4))
        rooted(0)
        for k in range(KT):
            act.wait_ge(scaled, k + 1)
            act.activation(H[:, k, :], MIX[:, k, :], ACT.Identity, bias=mod("sh_m0")[:, k:k + 1]).then_inc(h_ready, 1)
        def lora_group(L, g, quantity, bias, done):
            def make(dst, src):
                for j in range(4):
                    ins = act.activation(dst[:, j, :], src[:, T * j:T * j + T], ACT.Sigmoid,
                                         bias=pm(bias)[:, 4 * g + j:4 * g + j + 1])
                ins.then_inc(st_ready, 1)
            to_scratch(L, 4 * g, quantity, make, (lora_done, done))

        def plain(dst, src):
            act.activation(dst[:, :, :], src[:, :].rearrange("p (j t) -> p j t", j=4), ACT.Copy).then_inc(st_ready, 1)

        act.wait_ge(mix_used, KT)
        act.activation(TW[:, :], PT0[0:LORA, 0:T], ACT.Tanh).then_inc(lora_mid, 1)
        act.wait_ge(mix_used, 2 * KT)
        act.activation(AW[:, :], PT1[0:LORA, 0:T], ACT.Copy).then_inc(lora_mid, 1)
        for g in range(4):
            lora_group(g, g, 4, "w0", g + 1)
        act.wait_ge(mix_used, 3 * KT)
        act.activation(GW[:, :, :], PT0[:, :].rearrange("p (j t) -> p j t", j=2), ACT.Sigmoid).then_inc(lora_mid, 1)
        for g in range(4):
            lora_group(4 + g, g, 3, "a0", 5 + g)
        for g in range(4):
            to_scratch(8 + g, 4 * g, 5, plain, (lora_done, 9 + g))
        rounded(0)

        def mix_rounded(nm):
            q = nm % 4
            act.wait_ge(mix_full, nm + 1)
            if nm >= 4:
                act.wait_ge(panel_used, 16 * (nm // 4) - 4 + q + 1)
            act.activation(MH[:, 4 * q:4 * q + 4, :], MIX[:, 4 * q:4 * q + 4, :], ACT.Copy).then_inc(mh_ready, 1)

        for q in range(4):
            mix_rounded(q)
        for s, name in enumerate(("r", "k", "v")):
            st = stages[name]
            for g in range(4):
                for q in range(4):
                    rounded(st["p0"] + 4 * g + q + 1)
                    if g == 3 and q >= 1 and s < 2:
                        mix_rounded(4 * (s + 1) + q - 1)
                to_scratch(st["g0"] + g, 4 * g, s, plain, (panel_used, st["p0"] + 4 * g + 4))
            if s < 2:
                mix_rounded(4 * (s + 1) + 3)

        act.wait_ge(zeroed, 6)
        for stores in scr_stored:
            act.wait_ge(stores, 16 * 12)
        with act.Fori(0, KT // 2) as i:
            for tt in range(2):
                n = 2 * i + tt
                x = IN[tt]
                act.wait_ge(kkr_ready, n + 1)
                act.activation(KSQ[:, :], KKR[:, :], ACT.Square).then_inc(ksq_ready, 1)
                act.wait_ge(ss_done, n + 1)
                act.activation(KK[:, :], PS[:, 0:T], ACT.Sqrt).then_inc(nrm_ready, 1)
                act.wait_ge(cum_ready, n + 1)
                act.activation(WI[:, :], CUM[:, :], ACT.Exp, scale=-W_SCALE)
                act.activation(WV[:, :], CUM[:, :], ACT.Exp, scale=W_SCALE)
                act.activation(WE[:, :], CME[:, :], ACT.Exp, scale=-W_SCALE).then_inc(exp_ready, 1)
                for e in range(2):
                    h = slice(64 * e, 64 * e + 64)
                    act.activation(BDV[h, :, e, :], x[h, 2, :].rearrange("p (c t) -> p c t", c=NC), ACT.Copy)
                act.wait_ge(ar_ready, n + 1)
                act.wait_ge(b_ready, n + 1)
                for e in range(2):
                    h = slice(64 * e, 64 * e + 64)
                    act.activation(BDAR[h, :, :, e, :], AR[h, :, :, :], ACT.Copy)
                    ins = act.activation(BDB[h, :, e, :], BST[h, :, :], ACT.Copy)
                ins.then_inc(bd_ready, 1)
                act.wait_ge(scores_done, 3 * n + 3)
                act.activation(AST[:, :, :], PG[1][:, 0:T].rearrange("p (c t) -> p c t", c=NC), ACT.Copy)\
                   .then_inc(ast_ready, 1)
                act.wait_ge(tok_done, n + 1)
                act.activation(TOKV[:, :, :], PG[1][:, T:2 * T].rearrange("p (c t) -> p c t", c=NC), ACT.Copy)
                act.activation(TOKBK[:, :, :, :], PG[1][:, 2 * T:4 * T].rearrange("p (b c t) -> p b c t", b=2, c=NC),
                               ACT.Copy).then_inc(tok_ready, 1)
                for lv in range(5):
                    for hb in range(2):
                        k = 10 * n + 2 * lv + hb + 1
                        act.wait_ge(p_done, k)
                        act.activation(PC[:, 2 * hb:2 * hb + 2, :],
                                       PTT[hb][:, 0:2 * C].rearrange("p (c t) -> p c t", c=2), ACT.Copy)\
                           .then_inc(p_copied, 1)
                for c in range(NC):
                    k = NC * n + c + 1
                    act.wait_ge(rhs_done, k)
                    act.activation(RH[:, :], PT0[:, 0:C], ACT.Copy).then_inc(rhs_ready, 1)
                    act.wait_ge(u_done, k)
                    act.activation(UU[:, :], PT1[:, 0:C], ACT.Copy).then_inc(u_ready, 1)
                act.wait_ge(yc_ready, n + 1)
                act.activation(YQ[:, :, :], YC[:, :, :], ACT.Square).then_inc(yq_ready, 1)
                act.wait_ge(yo_ready, n + 1)
                act.activation(MH[:, bass.ds(n, 1), :], Y2[:, :].rearrange("p (a t) -> p a t", a=1), ACT.Copy)\
                   .then_inc(mh_ready, 1)

        def y_evacuation(st, g, squares_too=False):
            act.wait_ge(panel_used, st["p0"] + st["q"] * (g + 1))
            act.activation(Y[:, 4 * g:4 * g + 4, :], PG[(st["g0"] + g) % 2][:, :].rearrange("p (j t) -> p j t", j=4),
                           ACT.Copy).then_inc(y_ready, 1)

        def produce(st, g):
            for q in range(st["q"]):
                n = st["p0"] + st["q"] * g + q + 1
                if not isinstance(n, int) or n < PANELS:
                    if isinstance(n, int):
                        rounded(n)
                    else:
                        slot = (st["p0"] + q + 1) % 4
                        rounded(n, slot, 8 * n + (32 - 8 * slot))

        def ffn(l):
            for part in range(3):
                st = stages[f"gu{l}{part}"]
                h0 = sum(x for x, _ in PARTS[:part])
                hall = 22 * l + h0
                with act.Fori(0, st["groups"] // 2) as i:
                    for j in range(2):
                        g = 2 * i + j
                        produce(st, g)
                        act.wait_ge(panel_used, st["p0"] + 4 * g + 4)
                        act.wait_ge(hid_ready, hall + g + 1)
                        act.activation(SG[j][:, :, :], PG[(st["g0"] + j) % 2][:, 0:512]
                                       .rearrange("p (j t) -> p j t", j=2), ACT.Silu).then_inc(sg_ready, 1)
                        act.wait_ge(hid_ready, hall + g + 3)
                        act.activation(HH[:, bass.ds(2 * g, 2), :], HID[j][:, :, :], ACT.Copy).then_inc(hh_ready, 1)
                st = stages[f"down{l}{part}"]
                for g in range(4):
                    produce(st, g)
                    if part == 0:
                        y_evacuation(st, g)

        produced = stages["o"]
        for g in range(4):
            produce(produced, g)
            y_evacuation(produced, g)
        squares(Y, lambda q: (y_ready, q + 2))
        rooted(1)
        squares(X, lambda q: (x_ready, q + 1))
        rooted(2)
        shifted(16, "sh_f0", None)
        ffn(0)
        squares(Y, lambda q: (y_ready, 17))
        rooted(3)
        squares(X, lambda q: (x_ready, 4 + q + 1))
        rooted(4)
        shifted(32, "sh_kv", None)
        st = stages["kv"]
        produce(st, 0)
        act.wait_ge(panel_used, st["p0"] + 4)
        pg = PG[st["g0"] % 2][:, :].rearrange("p (j t) -> p j t", j=4)
        act.activation(KR[:, :, :], pg[:, 0:2, :], ACT.Copy).then_inc(kv_copied, 1)
        act.activation(VR2[:, :, :], pg[:, 2:4, :], ACT.Copy).then_inc(kv_copied, 1)
        shifted(48, "sh_m1", None)
        act.wait_ge(rope_ready, 1)
        act.activation(SIN[:, :], ANG[:, :], ACT.Sin)
        act.activation(COS[:, :], ANG[:, :], ACT.Sin, scale=0.5).then_inc(sin_ready, 1)
        st = stages["q"]
        for g in range(4):
            produce(st, g)
            act.wait_ge(panel_used, st["p0"] + 4 * g + 4)
            act.activation(QR[:, 4 * g:4 * g + 4, :], PG[(st["g0"] + g) % 2][:, :].rearrange("p (j t) -> p j t", j=4),
                           ACT.Copy).then_inc(q_copied, 1)
        act.wait_ge(kd_done, 1)
        act.activation(KD[:, :, :], PG[0][:, :].rearrange("p (g t) -> p g t", g=4), ACT.Copy).then_inc(kd_ready, 1)
        act.wait_ge(vw_done, 1)
        act.activation(VW[0:64, 0, :], PG[1][0:64, 0:T], ACT.Copy)
        act.activation(VW[:, 1:4, :], PG[1][:, T:4 * T].rearrange("p (n c) -> p n c", n=3), ACT.Copy).then_inc(vw_ready, 1)
        with act.Fori(0, KT // 2) as i:
            for tt in range(2):
                n = 2 * i + tt
                act.wait_ge(max_ready, n + 1)
                for w in range(NC):
                    lo = 64 if w == 0 else 0
                    act.activation(PR[tt][:, w, lo:P], PTT[tt][:, P * w + lo:P * w + P], ACT.Exp,
                                   bias=NM[tt][:, w:w + 1], scale=ATT_SCALE, accum_out=SU[tt][:, w:w + 1])
                act.activation(ES[tt][:, :], ES[tt][:, :], ACT.Exp).then_inc(prob_ready, 1)
                act.wait_ge(pt_done, n + 1)
                pt = PG[tt][:, 0:512].rearrange("p (w q) -> p w q", w=NC)
                act.activation(PT[tt][0:64, 0, :], pt[0:64, 0, :], ACT.Copy)
                act.activation(PT[tt][:, 1:4, :], pt[:, 1:4, :], ACT.Copy).then_inc(pt_ready, 1)
                act.wait_ge(o_done, n + 1)
                act.activation(MH[:, bass.ds(n, 1), :], PG[tt][:, 512:768].rearrange("p (a t) -> p a t", a=1),
                               ACT.Copy).then_inc(mh_ready, 1)
        st = stages["ao"]
        for g in range(4):
            produce(st, g)
            y_evacuation(st, g)
        squares(Y, lambda q: (y_ready, 21))
        rooted(5)
        squares(X, lambda q: (x_ready, 8 + q + 1))
        rooted(6)
        shifted(64, "sh_f1", None)
        ffn(1)
        squares(Y, lambda q: (y_ready, 33))
        rooted(7)
        for g in range(8):
            act.wait_ge(turned, g + 1)
            act.activation(XO[:, g // 4, 512 * (g % 4):512 * (g % 4) + 512], PTT[g % 2][:, :], ACT.Copy)\
               .then_inc(drained, 1)

    @block.tensor
    def _(pe):
        mm = pe.matmul

        def take_wait(o):
            mm(o, ONESB[:, :], ONESB[:, 0:1], start=True, stop=True)

        def reduce_unit(u):
            pe.wait_ge(ada_used, 16 * u + 16)
            for j in range(8):
                ins = mm(PA[:, j:j + 1], ACC[:, P * j:P * j + P], ONES[:, 0:1], start=True, stop=True)
            ins.then_inc(red_done, 1)

        def group(st, g, hi, lo, parity, moving):
            pg = PG[parity]
            for q in range(st["q"]):
                n = st["p0"] + st["q"] * g + q
                slot = (st["p0"] + (st["q"] * g if isinstance(g, int) else 0) + q) % 2
                pe.wait_ge(wh_ready, n + 1)
                moving(g, q)
                for t in range(4):
                    for k in range(4):
                        w = WH[slot][:, k, P * t:P * t + P]
                        o = pg[:, T * t:T * t + T]
                        first = q == 0 and k == 0 and t % 2 == 0
                        mm(o, w, hi[:, 4 * q + k, :], start=first, stop=False, skip_group_check=True)
                        mm(o, w, lo[:, 4 * q + k, :], start=False, stop=False, skip_group_check=True)
                pe.wait_ge(wl_ready, n + 1)
                pe.wait_ge(wlp_ready, n + 1)
                for t in range(4):
                    for k in range(4):
                        ins = mm(pg[:, T * t:T * t + T], WL[slot][:, k, P * t:P * t + P], hi[:, 4 * q + k, :],
                                 start=False, stop=(q == st["q"] - 1 and k == 3), skip_group_check=True)
                ins.then_inc(panel_used, 1)

        def square_sums_all(n):
            if n:
                pe.wait_ge(rt_ready, n)
            for q in range(4):
                pe.wait_ge(squared, 4 * n + q + 1)
                for k in range(4):
                    ins = mm(PS[:, 0:T], ONES[:, :], SQ[q % 2][:, k, :], start=(q == 0 and k == 0),
                             stop=(q == 3 and k == 3))
                ins.then_inc(sq_used, 1)

        pe.wait_ge(cst_full, 16)
        pe.wait_ge(par_full, 16 * 14)
        for b in range(5):
            r = P if b < 4 else 80
            ins = pe.transpose(PG[0][:, P * b:P * b + r], PROW[0:r, b, :], cst("ident")[0:r, 0:r])
        ins.then_inc(par_turned, 1)
        pe.wait_ge(ones_set, 2)
        reduce_unit(0)
        pe.wait_ge(x_full, 16)
        for g in range(4):
            if g == 0:
                pe.wait_ge(par_copied, 1)
            elif g >= 2:
                pe.wait_ge(x_copied, g - 1)
            for j in range(4):
                for h in range(2):
                    ins = pe.transpose(PG[g % 2][:, T * j + P * h:T * j + P * h + P],
                                       XIN[:, h, P * (4 * g + j):P * (4 * g + j) + P], cst("ident"))
            ins.then_inc(x_turned, 1)
        square_sums_all(0)
        for u in range(1, 4):
            reduce_unit(u)
        def lora_first(n, w, width, outs):
            for k in range(KT):
                pe.wait_ge(mix_ready, KT * n + k + 1)
                for j, o in enumerate(outs):
                    ins = mm(o, w(k, j), MIX[:, k, :], start=(k == 0 and j == 0), stop=(k == KT - 1),
                             skip_group_check=True)
                ins.then_inc(mix_used, 1)

        flat = lambda n: RAW[n][:, :, :].rearrange("p a b -> p (a b)")
        pe.wait_ge(lora_full[0], 16)
        lora_first(0, lambda k, j: flat(0)[:, LORA * k:LORA * k + LORA], LORA, [PT0[0:LORA, 0:T]])
        pe.wait_ge(lora_full[1], 16)
        lora_first(1, lambda k, j: flat(1)[:, LORA * k:LORA * k + LORA], LORA, [PT1[0:LORA, 0:T]])
        done = [0]

        def lora_second(mid, full, make):
            pe.wait_ge(lora_mid, mid)
            for w, v in full:
                pe.wait_ge(w, v)
            for g in range(4):
                gi = done[0]
                if gi >= 2:
                    pe.wait_ge(st_ready, gi - 1)
                for t in range(4):
                    ins = make(PG[gi % 2][:, T * t:T * t + T], 4 * g + t, t % 2 == 0)
                ins.then_inc(lora_done, 1)
                done[0] += 1

        lora_second(1, [(lora_full[0], 32)],
                    lambda o, j, first: mm(o, flat(0)[0:LORA, P * j:P * j + P], TW[:, :], start=first, stop=True,
                                           skip_group_check=True))
        pe.wait_ge(lora_full[2], 16)
        pe.wait_ge(lora_full[3], 16)
        g1 = [RAW[2 + n][:, :, :].rearrange("p a (b n) -> p (a b) n", b=2) for n in range(2)]
        lora_first(2, lambda k, j: g1[k // 8][:, k % 8, P * j:P * j + P], 0, [PT0[:, 0:T], PT0[:, T:2 * T]])
        lora_second(2, [(lora_full[1], 32)],
                    lambda o, j, first: mm(o, flat(1)[0:LORA, P * j:P * j + P], AW[:, :], start=first, stop=True,
                                           skip_group_check=True))

        def gate_second(o, j, first):
            mm(o, flat(2)[:, P * j:P * j + P], GW[:, 0, :], start=first, stop=False, skip_group_check=True)
            return mm(o, flat(3)[:, P * j:P * j + P], GW[:, 1, :], start=False, stop=True, skip_group_check=True)

        lora_second(3, [(lora_full[2], 32), (lora_full[3], 32)], gate_second)

        for s, name in enumerate(("r", "k", "v")):
            def moving(g, q, s=s):
                pe.wait_ge(mh_ready, 4 * s + q + 1)
                pe.wait_ge(ml_ready, 4 * s + q + 1)
            st = stages[name]
            with pe.Fori(0, 2) as i:
                for j in range(2):
                    pe.wait_ge(st_ready, 12 + 4 * s + 2 * i + j - 1)
                    group(st, 2 * i + j, MH, ML, j, moving)

        sid = cst("stacked_ident")
        pe.wait_ge(st_ready, 24)
        pe.wait_ge(zeroed, 6)
        with pe.Fori(0, KT // 2) as i:
            for tt in range(2):
                n = 2 * i + tt
                pe.wait_ge(ksq_ready, n + 1)
                pe.wait_ge(mh_ready, 12 + n)
                mm(PS[:, 0:T], cst("head_ones"), KSQ[:, :], start=True, stop=True).then_inc(ss_done, 1)
                pe.wait_ge(rr_ready, n + 1)
                pe.wait_ge(nrm_ready, n + 1)
                mm(PS[:, T:2 * T], cst("head_ones"), RR[:, :], start=True, stop=True).then_inc(bonus_used, 1)
                pe.wait_ge(bd_ready, n + 1)
                pe.wait_ge(bdk_ready, n + 1)
                for c in range(NC):
                    ins = mm(PG[0][:, P * c:P * c + P], BDB[:, c, :, :], AR[:, c, :, :], start=True, stop=True)
                ins.then_inc(scores_done, 1)
                for c in range(NC):
                    ins = mm(PG[0][:, 512 + P * c:512 + P * c + P], BDK[:, c, :, :], AR[:, c, :, :], start=True, stop=True)
                ins.then_inc(scores_done, 1)
                for c in range(NC):
                    mm(PG[1][:, C * c:C * c + C], BDAR[:, c, 0, :, :], BST[:, c, :], start=True, stop=True)
                    ins = mm(PG[1][:, T + C * c:T + C * c + C], BDV[:, c, :, :], sid, start=True, stop=True)
                ins.then_inc(scores_done, 1)
                for c in range(NC):
                    mm(PG[1][:, 2 * T + C * c:2 * T + C * c + C], BDB[:, c, :, :], sid, start=True, stop=True)
                for c in range(NC):
                    ins = mm(PG[1][:, 3 * T + C * c:3 * T + C * c + C], BDK[:, c, :, :], sid, start=True, stop=True)
                ins.then_inc(tok_done, 1)
                pe.wait_ge(coef_ready, n + 1)
                for lv in range(5):
                    for hb in range(2):
                        k = 2 * lv + hb
                        pe.wait_ge(nt_ready, 9 * n + (1 if lv == 0 else 2 * lv + hb))
                        pe.wait_ge(am_ready, 5 * n + lv + 1)
                        take_wait(PTT[hb][:, 256:257])
                        for c in range(2):
                            for e in range(2):
                                h = slice(64 * e, 64 * e + 64)
                                ins = mm(PTT[hb][h, C * c:C * c + C], AM[lv % 2][h, 2 * hb + c, :],
                                         NT[h, 2 * hb + c, 0, :], start=True, stop=True)
                        ins.then_inc(p_done, 1)
                    for hb in range(2):
                        pe.wait_ge(p_copied, 10 * n + 2 * lv + hb + 1)
                        take_wait(PG[0][:, 512 * hb + 511:512 * hb + 512])
                        for c in range(2):
                            cc = 2 * hb + c
                            for e in range(2):
                                h = slice(64 * e, 64 * e + 64)
                                o = 512 * hb + 2 * C * c
                                ins = mm(PG[0][h, o:o + C], NT[h, cc, 1, :], PC[h, cc, :], start=True, stop=True)
                                if lv < 4:
                                    ins = mm(PG[0][h, o + C:o + 2 * C], PC[h, cc, :], NT[h, cc, 1, :],
                                             start=True, stop=True)
                        ins.then_inc(d_done, 1)
                pe.wait_ge(tok_ready, n + 1)
                pe.wait_ge(nbd_ready, n + 1)
                for c in range(NC):
                    k = NC * n + c
                    ins = mm(PT0[:, 0:C], AAK[:, c, :, :], TOKV[:, c, :], start=True, stop=(c == 0))
                    if c:
                        pe.wait_ge(s_ready, 3 * n + c)
                        ins = mm(PT0[:, 0:C], BDAR[:, c, 0, :, :], SS[:, :], start=False, stop=True)
                    ins.then_inc(rhs_done, 1)
                    pe.wait_ge(rhs_ready, k + 1)
                    mm(PT1[:, 0:C], NBD[:, c, :, :], RH[:, :], start=True, stop=True).then_inc(u_done, 1)
                    pe.wait_ge(u_ready, k + 1)
                    if c < NC - 1:
                        take_wait(PG[1][:, 511:512])
                        for e in range(2):
                            h = slice(64 * e, 64 * e + 64)
                            mm(PG[1][h, 0:C], TOKBK[h, 0, c, :], UU[h, :], start=True, stop=False)
                            ins = mm(PG[1][h, 0:C], TOKBK[h, 1, c, :], TOKV[h, c, :], start=False, stop=True)
                        ins.then_inc(sd_done, 1)
                    yo = PG[1][:, 512 + C * c:512 + C * c + C]
                    if c:
                        mm(yo, BDAR[:, c, 1, :, :], SS[:, :], start=True, stop=False)
                    mm(yo, ARB[:, c, :, :], UU[:, :], start=(c == 0), stop=False)
                    mm(yo, ARK[:, c, :, :], TOKV[:, c, :], start=False, stop=True).then_inc(y_done, 1)
                pe.wait_ge(ybd_ready, n + 1)
                for c in range(NC):
                    ins = mm(PS[:, C * c:C * c + C], YBD[:, c, :, :], sid, start=True, stop=True)
                ins.then_inc(yt_done, 1)
            reduce_unit(i + 4)

        def output_stage(name, hi, lo, moving, free):
            st = stages[name]
            p = st["g0"] % 2
            if st["q"] == 4:
                with pe.Fori(0, 2) as i:
                    for j in range(2):
                        if name == "o":
                            pe.wait_ge(y_ready, 2 * i + 1 if j else i + 1)
                        else:
                            free(2 * i + j, j)
                        group(st, 2 * i + j, hi, lo, (p + j) % 2, moving)
                    if name in CARRY:
                        reduce_unit(i + CARRY[name])
            else:
                for g in range(4):
                    free(g, g)
                    group(st, g, hi, lo, (p + g) % 2, moving)

        def by_tile(base):
            def moving(g, q):
                pe.wait_ge(mh_ready, base + 4 * q + 4)
                pe.wait_ge(ml_ready, base + 4 * q + 4)
            return moving

        YB = [4, 20]

        def ffn(l):
            base = 28 if l == 0 else 92
            for part in range(3):
                st = stages[f"gu{l}{part}"]
                h0 = 22 * l + sum(x for x, _ in PARTS[:part])
                if part:
                    pe.wait_ge(y_ready, YB[l] + 4 * part + 1)
                with pe.Fori(0, st["groups"] // 2) as i:
                    for j in range(2):
                        g = 2 * i + j
                        pe.wait_ge(hid_ready, h0 + g + 1)
                        group(st, g, MH, ML, (st["g0"] + j) % 2, by_tile(base))
                    if st["name"] in CARRY:
                        reduce_unit(i + CARRY[st["name"]])

                def moving(g, q, h0=h0):
                    pe.wait_ge(hh_ready, h0 + 2 * q + 2)
                    pe.wait_ge(hl_ready, h0 + 2 * q + 4)

                n0 = YB[l] + 4 * part
                last = h0 + st["groups"]

                def free(g, j, n0=n0, last=last):
                    pe.wait_ge(hid_ready, last + (2 if j else 1))
                    if isinstance(g, int):
                        if g >= 2:
                            pe.wait_ge(y_ready, n0 + g)
                    else:
                        pe.wait_ge(y_ready, n0 + g)

                output_stage(f"down{l}{part}", HH, HL, moving, free)

        st = stages["o"]
        pe.wait_ge(ml_ready, 12 + KT)
        output_stage("o", MH, ML, by_tile(12), lambda g, j: None)
        square_sums_all(1)
        square_sums_all(2)
        ffn(0)
        square_sums_all(3)
        square_sums_all(4)
        st = stages["kv"]
        group(st, 0, MH, ML, st["g0"] % 2, by_tile(44))
        reduce_unit(23)

        pe.wait_ge(kv_copied, 2)
        st = stages["q"]
        with pe.Fori(0, 2) as i:
            for j in range(2):
                pe.wait_ge(q_copied, 2 * i + 1 if j else i + 1)
                group(st, 2 * i + j, MH, ML, (st["g0"] + j) % 2, by_tile(60))
            reduce_unit(i + CARRY["q"])
        pe.wait_ge(q_copied, 5)
        mm(PT0[:, :], cst("rope_swap"), KR[:, :, :], start=True, stop=True).then_inc(swap_done, 1)
        pe.wait_ge(roped, 1)
        for g in range(4):
            ins = mm(PG[0][:, T * g:T * g + T], cst(f"dup{g % 2}"), KX[:, g // 2, :], start=(g % 2 == 0), stop=True,
                     skip_group_check=True)
        ins.then_inc(kd_done, 1)
        for w in range(NC):
            lo, m = (0, 64) if w == 0 else (64 * (w - 1), P)
            for j in range(2):
                ins = pe.transpose(PG[1][0:m, T * w + P * j:T * w + P * j + P], VR2[:, j, lo:lo + m], cst("ident"))
        ins.then_inc(vw_done, 1)
        pe.wait_ge(kd_ready, 1)
        pe.wait_ge(vw_ready, 1)
        for g in range(4):
            with pe.Fori(0, 2) as i:
                for tt in range(2):
                    n = 2 * i + tt + 4 * g
                    pe.wait_ge(roped, n + 1)
                    mm(PTT[tt][:, 0:T], cst("rope_swap"), QR[:, bass.ds(n, 1), :], start=True, stop=True)\
                      .then_inc(swap_done, 1)
                    pe.wait_ge(roped, n + 2)
                    take_wait(PTT[tt][:, 0:1])
                    for w in range(NC):
                        lo = 64 * w - 64 if w else 0
                        for e in range(2):
                            h = slice(64 * e, 64 * e + 64)
                            if w == 0:
                                ins = mm(PTT[tt][h, 64:P], QS[tt][h, 0:64], KD[h, g, 0:64], start=True, stop=True)
                            else:
                                ins = mm(PTT[tt][h, P * w:P * w + P], QS[tt][h, 64 * w:64 * w + 64],
                                         KD[h, g, lo:lo + P], start=True, stop=True)
                    ins.then_inc(sco_done, 1)
                    pe.wait_ge(norm_ready, n + 1)
                    for w in (1, 2, 3, 0):
                        m = 64 if w == 0 else P
                        ins = pe.transpose(PG[tt][0:m, P * w:P * w + P], PR[tt][:, w, P - m:P], cst("ident"))
                    ins.then_inc(pt_done, 1)
                    pe.wait_ge(pt_ready, n + 1)
                    for w in (1, 2, 3, 0):
                        m = 64 if w == 0 else P
                        for e in range(2):
                            ins = mm(PG[tt][64 * e:64 * e + 64, 512 + C * w:512 + C * w + C], VW[0:m, w, C * g:C * g + C],
                                     PT[tt][0:m, w, C * e:C * e + C], start=True, stop=True)
                    ins.then_inc(o_done, 1)
        pe.wait_ge(ml_ready, 92)
        output_stage("ao", MH, ML, by_tile(76), lambda g, j: pe.wait_ge(y_ready, 16 + g))
        square_sums_all(5)
        square_sums_all(6)
        ffn(1)
        square_sums_all(7)
        pe.wait_ge(x_ready, 16)
        for g in range(8):
            if g >= 2:
                pe.wait_ge(drained, g - 1)
            for j in range(4):
                k = 4 * (g % 4) + j
                ins = pe.transpose(PTT[g % 2][:, P * j:P * j + P], X[:, k, P * (g // 4):P * (g // 4) + P], cst("ident"))
            ins.then_inc(turned, 1)

    @block.vector
    def _(dve):
        step = Tally(v_step)

        def link(ins):
            dve.wait_ge(v_step, step.add(ins))

        def residue(n, slot=None):
            if isinstance(n, int):
                slot = n % 4
            dve.wait_ge(wh_ready, n + 1)
            if not (isinstance(n, int) and n < 2):
                dve.wait_ge(panel_used, n - 1)
            dve.tensor_tensor(WL[slot % 2][:, 0:2, :], RAW[slot][:, 0:2, :], WH[slot % 2][:, 0:2, :].bitcast(F32),
                              ALU.subtract).then_inc(wl_ready, 1)

        def ada_step(u, s):
            m = 16 * u + s
            dve.wait_ge(ada_full[s % 4], 16 * (4 * u + s // 4) + 16)
            if s == 0:
                if not (isinstance(u, int) and u == 0):
                    dve.wait_ge(red_done, u)
                dve.tensor_scalar(ACC[:, :], ADA[0][:, :], CA[:, 0:1], None, ALU.mult).then_inc(ada_used, 1)
            else:
                dve.wait_ge(ada_used, m)
                ins = dve.scalar_tensor_tensor(out=ACC[:, :], in0=ADA[s % 4][:, :], scalar=CA[:, s:s + 1],
                                               in1=ACC[:, :], op0=ALU.mult, op1=ALU.add)
                ins.then_inc(ada_used, 1)

        def ada_finish(u):
            dve.wait_ge(red_done, u + 1)
            dve.tensor_tensor(MODS[:, bass.ds(8 * u, 8)], PA[:, 0:8], PM[:, bass.ds(col["bias"] + 8 * u, 8)], ALU.add)\
               .then_inc(mods_ready, 1)

        def inverse_rms(n):
            dve.wait_ge(rt_ready, n + 1)
            dve.reciprocal(RS[:, :], RT[:, :]).then_inc(rs_ready, 1)
            dve.wait_ge(rs_ready, n + 1)

        def gains(scale, g, units):
            dve.wait_ge(mods_ready, units)
            link(dve.scalar_tensor_tensor(out=SV[:, :], in0=mod(scale), scalar=1.0, in1=pm(g), op0=ALU.add, op1=ALU.mult))

        def residual(n, gate, g, nx, units):
            dve.wait_ge(mods_ready, units)
            link(dve.tensor_tensor(GG[:, :], mod(gate), pm(g), ALU.mult))
            inverse_rms(n)
            for q in range(4):
                for k in range(4 * q, 4 * q + 4):
                    ins = dve.scalar_tensor_tensor(out=Y[:, k, :], in0=Y[:, k, :], scalar=GG[:, k:k + 1],
                                                   in1=RS[:, :], op0=ALU.mult, op1=ALU.mult)
                link(ins)
                dve.tensor_tensor(X[:, 4 * q:4 * q + 4, :], X[:, 4 * q:4 * q + 4, :], Y[:, 4 * q:4 * q + 4, :], ALU.add)\
                   .then_inc(x_ready, 1)
            dve.wait_ge(x_ready, nx + 4)

        def modulated(nh, nm, shift):
            for k in range(KT):
                dve.scalar_tensor_tensor(out=Y[:, k, :], in0=X[:, k, :], scalar=SV[:, k:k + 1], in1=RS[:, :],
                                         op0=ALU.mult, op1=ALU.mult).then_inc(scaled, 1)
                if k:
                    low(nm, k - 1, shift)
            low(nm, KT - 1, shift)

        def low(nm, k, shift):
            dve.wait_ge(mh_ready, nm + k + 1)
            dve.scalar_tensor_tensor(out=ML[:, k, :], in0=Y[:, k, :], scalar=mod(shift)[:, k:k + 1],
                                     in1=MH[:, k, :].bitcast(F32), op0=ALU.add, op1=ALU.subtract).then_inc(ml_ready, 1)

        dve.memset(GG[:, 0:1], 0.0).then_inc(hid_ready, 1)
        dve.memset(GG[:, 1:2], 0.0).then_inc(hid_ready, 1)
        dve.memset(GG[:, 2:3], 0.0).then_inc(hl_ready, 1)
        dve.memset(GG[:, 3:4], 0.0).then_inc(hl_ready, 1)
        dve.memset(GG[:, 4:5], 0.0).then_inc(y_ready, 1)
        dve.memset(GG[:, 5:6], 0.0).then_inc(q_copied, 1)
        dve.wait_ge(par_copied, 1)
        link(dve.tensor_scalar(OMK[:, :], pm("k_a"), -1.0, 1.0, ALU.mult, ALU.add))
        dve.wait_ge(ca_ready, 1)
        for u in range(4):
            for s in range(16):
                ada_step(u, s)
            ada_finish(u)
        gains("sc_m0", "g00", 4)
        inverse_rms(0)
        dve.wait_ge(x_turned, 4)
        for k in range(KT):
            dve.scalar_tensor_tensor(out=MIX[:, k, :], in0=X[:, k, :], scalar=SV[:, k:k + 1], in1=RS[:, :],
                                     op0=ALU.mult, op1=ALU.mult).then_inc(scaled, 1)
        dve.wait_ge(h_ready, KT)
        dve.tensor_tensor(XX[:, :, 1:T], H[:, :, 0:T - 1], H[:, :, 1:T], ALU.subtract)
        link(dve.tensor_scalar(XX[:, :, 0:1], H[:, :, 0:1], -1.0, None, ALU.mult))
        for n, i in enumerate((1, 4, 5)):
            for k in range(KT):
                if n:
                    dve.wait_ge(mix_used, KT * (n - 1) + k + 1)
                dve.scalar_tensor_tensor(out=MIX[:, k, :], in0=XX[:, k, :], scalar=pm(f"mu{i}")[:, k:k + 1],
                                         in1=H[:, k, :], op0=ALU.mult, op1=ALU.add).then_inc(mix_ready, 1)

        def mixture(nm):
            q, s = nm % 4, nm // 4
            if s == 0:
                dve.wait_ge(mix_used, 2 * KT + 4 * q + 4)
            else:
                dve.wait_ge(ml_ready, nm - 3)
            for k in range(4 * q, 4 * q + 4):
                ins = dve.scalar_tensor_tensor(out=MIX[:, k, :], in0=XX[:, k, :],
                                               scalar=pm(f"mu{(0, 2, 3)[s]}")[:, k:k + 1], in1=H[:, k, :],
                                               op0=ALU.mult, op1=ALU.add)
            ins.then_inc(mix_full, 1)
            dve.wait_ge(mh_ready, nm + 1)
            dve.tensor_tensor(ML[:, 4 * q:4 * q + 4, :], MIX[:, 4 * q:4 * q + 4, :],
                              MH[:, 4 * q:4 * q + 4, :].bitcast(F32), ALU.subtract).then_inc(ml_ready, 1)

        residue(0)
        for q in range(4):
            mixture(q)
        for s, name in enumerate(("r", "k", "v")):
            st = stages[name]
            for g in range(4):
                for q in range(4):
                    residue(st["p0"] + 4 * g + q + 1)
                    if g == 3 and q >= 1 and s < 2:
                        mixture(4 * (s + 1) + q - 1)
            if s < 2:
                mixture(4 * (s + 1) + 3)

        dve.wait_ge(zeroed, 6)
        for stores in scr_stored:
            dve.wait_ge(stores, 16 * 12)
        bc = lambda x, *shape: x.to_broadcast([P, *shape])
        LINKS = SCAN_LINKS
        base_step = step.v
        c4 = lambda x: x.rearrange("p (c t) -> p c t", c=NC)
        with dve.Fori(0, KT // 2) as i:
            step.v, step.k = base_step + i * (2 * LINKS), 0
            for tt in range(2):
                n = 2 * i + tt
                r, k, v, aa, sw, g = (IN[tt][:, x, :] for x in range(6))
                vec = lambda name: PM[:, bass.ds(col[name] + n, 1)]
                unit_steps = iter([8 * tt + s for s in range(8)])
                carry = lambda: ada_step(i + 4, next(unit_steps))
                dve.wait_ge(in_full[tt], 16 * i + 16)
                dve.tensor_scalar(KKR[:, :], k, vec("k_k"), None, ALU.mult).then_inc(kkr_ready, 1)
                link(dve.tensor_tensor_scan(CUM[:, :], cst("carry"), sw, 0.0, ALU.mult, ALU.add))
                dve.tensor_tensor(CME[:, :], CUM[:, :], sw, ALU.subtract).then_inc(cum_ready, 1)
                link(dve.tensor_scalar(T1[:, :], aa, vec("k_a"), OMK[:, bass.ds(n, 1)], ALU.mult, ALU.add))
                link(dve.tensor_tensor(KP[:, :], k, T1[:, :], ALU.mult))
                dve.scalar_tensor_tensor(out=RR[:, :], in0=r, scalar=vec("r_k"), in1=KP[:, :], op0=ALU.mult,
                                         op1=ALU.mult).then_inc(rr_ready, 1)
                dve.wait_ge(nrm_ready, n + 1)
                link(dve.tensor_scalar(T1[:, :], KK[:, :], 1e-12, None, ALU.max))
                link(dve.reciprocal(KK[:, :], T1[:, :]))
                link(dve.tensor_tensor(KK[:, :], KKR[:, :], KK[:, :], ALU.mult))
                link(dve.tensor_tensor(KKA[:, :], KK[:, :], aa, ALU.mult))
                dve.wait_ge(exp_ready, n + 1)
                dve.scalar_tensor_tensor(out=AR[:, :, 0, :], in0=c4(KK[:, :]), scalar=-1.0, in1=c4(WE[:, :]),
                                         op0=ALU.mult, op1=ALU.mult)
                dve.tensor_tensor(AR[:, :, 1, :], c4(r), c4(WI[:, :]), ALU.mult).then_inc(ar_ready, 1)
                dve.tensor_tensor(BST[:, :, :], c4(KKA[:, :]), c4(WV[:, :]), ALU.mult).then_inc(b_ready, 1)
                for e in range(2):
                    h = slice(64 * e, 64 * e + 64)
                    ins = dve.tensor_tensor(BDK[h, :, e, :], c4(KP[h, :]), c4(WV[h, :]), ALU.mult)
                ins.then_inc(bdk_ready, 1)
                dve.wait_ge(bonus_used, n + 1)
                link(dve.tensor_tensor(BV[:, :], PS[:, T:2 * T], v, ALU.mult))
                carry()
                pb = PG[0][:, 0:512].rearrange("p (c x t) -> p c x t", c=NC, x=2)
                pk = PG[0][:, 512:1024].rearrange("p (c x t) -> p c x t", c=NC, x=2)
                mask = lambda name: cst(name).unsqueeze(1)
                dve.wait_ge(scores_done, 3 * n + 1)
                dve.tensor_tensor(NT[:, :, 0, :], pb[:, :, 0, :], bc(mask("upper1"), NC, C), ALU.mult)
                bdm = lambda name: cst(name).rearrange("p (e t) -> p e t", e=2).unsqueeze(1).to_broadcast([P, NC, 2, C])
                dve.tensor_tensor(ARB[:, :, :, :], pb[:, :, 1:2, :].to_broadcast([P, NC, 2, C]), bdm("incl"), ALU.mult)
                dve.wait_ge(scores_done, 3 * n + 2)
                dve.tensor_tensor(AAK[:, :, :, :], pk[:, :, 0:1, :].to_broadcast([P, NC, 2, C]), bdm("strict"), ALU.mult)
                dve.tensor_tensor(ARK[:, :, :, :], pk[:, :, 1:2, :].to_broadcast([P, NC, 2, C]), bdm("incl"), ALU.mult)\
                   .then_inc(coef_ready, 1)
                dve.wait_ge(ast_ready, n + 1)
                link(dve.tensor_tensor(NT[:, :, 1, :], AST[:, :, :], bc(mask("lower1"), NC, C), ALU.mult))
                dve.tensor_tensor(NT[:, :, :, :], NT[:, :, :, :],
                                  cst("stacked_ident").unsqueeze(1).unsqueeze(1).to_broadcast([P, NC, 2, C]), ALU.add).then_inc(nt_ready, 1)
                def level_mask(lv):
                    dve.tensor_tensor(AM[lv % 2][:, :, :], AST[:, :, :], bc(mask(f"lower{LEVELS[lv]}"), NC, C),
                                      ALU.mult).then_inc(am_ready, 1)

                level_mask(0)
                for lv in range(5):
                    if lv < 4:
                        level_mask(lv + 1)
                    carry()
                    for hb in range(2):
                        dve.wait_ge(d_done, 10 * n + 2 * lv + hb + 1)
                        cs = slice(2 * hb, 2 * hb + 2)
                        pd = PG[0][:, 512 * hb:512 * hb + 4 * C].rearrange("p (c x t) -> p c x t", c=2, x=2)
                        if lv < 4:
                            dve.tensor_tensor(NT[:, cs, :, :], NT[:, cs, :, :], pd, ALU.add).then_inc(nt_ready, 1)
                        else:
                            for e in range(2):
                                h = slice(64 * e, 64 * e + 64)
                                ins = dve.tensor_tensor(NBD[h, cs, e, :], pd[h, :, 0, :], NT[h, cs, 0, :], ALU.add)
                            if hb == 1:
                                ins.then_inc(nbd_ready, 1)
                for c in range(NC - 1):
                    wc = WI[:, C * c + C - 1:C * c + C]
                    if c:
                        link(dve.tensor_scalar(SW[:, :], SS[:, :], wc, None, ALU.mult))
                    dve.wait_ge(sd_done, 3 * n + c + 1)
                    if c:
                        dve.wait_ge(y_done, 4 * n + c + 1)
                        dve.scalar_tensor_tensor(out=SS[:, :], in0=PG[1][:, 0:C], scalar=wc, in1=SW[:, :],
                                                 op0=ALU.mult, op1=ALU.add).then_inc(s_ready, 1)
                    else:
                        dve.tensor_scalar(SS[:, :], PG[1][:, 0:C], wc, None, ALU.mult).then_inc(s_ready, 1)
                    dve.wait_ge(s_ready, 3 * n + c + 1)
                    if c < 2:
                        carry()
                py = c4(PG[1][:, 512:768])
                dve.wait_ge(y_done, 4 * n + 4)
                link(dve.tensor_reduce(MS[:, :], py, AX.X, ALU.add))
                link(dve.tensor_scalar(MS[:, :], MS[:, :], 1.0 / C, None, ALU.mult))
                dve.tensor_tensor(YC[:, :, :], py, bc(MS[:, :].unsqueeze(2), NC, C), ALU.subtract).then_inc(yc_ready, 1)
                dve.wait_ge(yq_ready, n + 1)
                link(dve.tensor_reduce(MS[:, :], YQ[:, :, :], AX.X, ALU.add))
                dve.tensor_scalar(VS[:, :], MS[:, :], 1.0 / C, GN_EPS, ALU.mult, ALU.add).then_inc(vs_ready, 1)
                dve.wait_ge(vr_ready, n + 1)
                for e in range(2):
                    h = slice(64 * e, 64 * e + 64)
                    ins = dve.tensor_tensor(YBD[h, :, e, :], YC[h, :, :], VR[h, :].unsqueeze(2).to_broadcast([64, NC, C]),
                                            ALU.mult)
                ins.then_inc(ybd_ready, 1)
                dve.wait_ge(yt_done, n + 1)
                link(dve.tensor_scalar(Y2[:, :], PS[:, 0:T], vec("gn_g"), vec("gn_b"), ALU.mult, ALU.add))
                link(dve.tensor_tensor(Y2[:, :], Y2[:, :], BV[:, :], ALU.add))
                dve.tensor_tensor(Y2[:, :], Y2[:, :], g, ALU.mult).then_inc(yo_ready, 1)
                dve.wait_ge(mh_ready, 12 + n + 1)
                y3 = Y2[:, :].rearrange("p (a t) -> p a t", a=1)
                dve.tensor_tensor(ML[:, bass.ds(n, 1), :], y3, MH[:, bass.ds(n, 1), :].bitcast(F32), ALU.subtract)\
                   .then_inc(ml_ready, 1)
                dve.wait_ge(ml_ready, 12 + n + 1)
            assert step.k == 2 * LINKS, step.k
            ada_finish(i + 4)
        step.v = base_step + (KT // 2) * 2 * LINKS

        def produce(st, g, u=None, odd=False):
            for q in range(st["q"]):
                n = st["p0"] + st["q"] * g + q + 1
                if not isinstance(n, int):
                    residue(n, (st["p0"] + q + 1) % 4)
                elif n < PANELS:
                    residue(n)
                if u is not None:
                    per = 4 if st["name"] == "kv" else 2
                    for s in range(per):
                        ada_step(u, per * q + s + (8 if odd else 0))

        def carried(st, i):
            return i + CARRY[st["name"]] if st["name"] in CARRY else None

        def ffn(l):
            for part in range(3):
                st = stages[f"gu{l}{part}"]
                hall = 22 * l + sum(x for x, _ in PARTS[:part])
                with dve.Fori(0, st["groups"] // 2) as i:
                    for j in range(2):
                        g = 2 * i + j
                        produce(st, g, carried(st, i), j == 1)
                        dve.wait_ge(sg_ready, hall + g + 1)
                        dve.wait_ge(hl_ready, hall + g + 1)
                        dve.tensor_tensor(HID[j][:, :, :], SG[j][:, :, :], PG[(st["g0"] + j) % 2][:, 512:1024]
                                          .rearrange("p (j t) -> p j t", j=2), ALU.mult).then_inc(hid_ready, 1)
                        dve.wait_ge(hh_ready, hall + g + 1)
                        dve.tensor_tensor(HL[:, bass.ds(2 * g, 2), :], HID[j][:, :, :],
                                          HH[:, bass.ds(2 * g, 2), :].bitcast(F32), ALU.subtract).then_inc(hl_ready, 1)
                    if st["name"] in CARRY:
                        ada_finish(carried(st, i))
                st = stages[f"down{l}{part}"]
                for g in range(4):
                    produce(st, g)
                    if part:
                        dve.wait_ge(panel_used, st["p0"] + st["q"] * (g + 1))
                        y = Y[:, 4 * g:4 * g + 4, :]
                        dve.wait_ge(y_ready, (5 if l == 0 else 21) + 4 * part)
                        dve.tensor_tensor(y, y, PG[(st["g0"] + g) % 2][:, :].rearrange("p (j t) -> p j t", j=4),
                                          ALU.add).then_inc(y_ready, 1)

        for g in range(4):
            produce(stages["o"], g)
        residual(1, "g_m0", "g01", 0, 12)
        gains("sc_f0", "g02", 12)
        inverse_rms(2)
        modulated(16, 28, "sh_f0")
        ffn(0)
        residual(3, "g_f0", "g03", 4, 16)
        gains("sc_kv", "kvg", 16)
        inverse_rms(4)
        modulated(32, 44, "sh_kv")
        st = stages["kv"]
        produce(st, 0, 23)
        ada_finish(23)
        dve.wait_ge(ml_ready, 60)
        gains("sc_m1", "g10", 20)
        dve.wait_ge(panel_used, st["p0"] + 4)
        modulated(48, 60, "sh_m1")
        dve.wait_ge(att_full, 32)
        for e in range(2):
            h = slice(64 * e, 64 * e + 64)
            link(dve.tensor_copy(SNK[h, :], SNKA[h, :].rearrange("p (j e) -> p e j", e=2)[:, e, :]))
        link(dve.tensor_copy(TURN[:, :], POSI[:, :]))
        link(dve.tensor_scalar(ANG[:, :], TURN[:, :], cst("freq"), None, ALU.mult))
        link(dve.tensor_scalar(TURN[:, :], ANG[:, :], float(1 / (2 * np.pi)), None, ALU.mult))
        link(dve.tensor_scalar(TURN[:, :], TURN[:, :], MAGIC, None, ALU.add))
        link(dve.tensor_scalar(TURN[:, :], TURN[:, :], -MAGIC, None, ALU.add))
        link(dve.scalar_tensor_tensor(out=ANG[:, :], in0=TURN[:, :], scalar=-TWO_PI_HI, in1=ANG[:, :],
                                      op0=ALU.mult, op1=ALU.add))
        link(dve.scalar_tensor_tensor(out=ANG[:, :], in0=TURN[:, :], scalar=-TWO_PI_LO, in1=ANG[:, :],
                                      op0=ALU.mult, op1=ALU.add))
        dve.tensor_scalar(ANG[:, :], ANG[:, :], -3.1415925, 3.1415925, ALU.max, ALU.min).then_inc(rope_ready, 1)
        dve.wait_ge(sin_ready, 1)
        link(dve.tensor_scalar(SIN[:, :], SIN[:, :], cst("rope_sign"), None, ALU.mult))
        link(dve.tensor_tensor(COS[:, :], COS[:, :], COS[:, :], ALU.mult))
        link(dve.tensor_scalar(COS[:, :], COS[:, :], -2.0, 1.0, ALU.mult, ALU.add))
        st = stages["q"]
        for g in range(4):
            produce(st, g, CARRY["q"] + g // 2, g % 2 == 1)
            if g % 2:
                ada_finish(CARRY["q"] + g // 2)
        two = lambda x: x.unsqueeze(1).to_broadcast([P, 2, T])
        dve.wait_ge(kv_copied, 2)
        dve.wait_ge(swap_done, 1)
        link(dve.tensor_tensor(KX[:, :, :], PT0[:, :].rearrange("p (j t) -> p j t", j=2), two(SIN[:, :]), ALU.mult))
        link(dve.tensor_tensor(KR[:, :, :], KR[:, :, :], two(COS[:, :]), ALU.mult))
        dve.tensor_tensor(KX[:, :, :], KX[:, :, :], KR[:, :, :], ALU.add).then_inc(roped, 1)
        dve.wait_ge(q_copied, 5)
        base_step = step.v
        with dve.Fori(0, KT // 2) as i:
            step.v, step.k = base_step + i * (2 * ATT_LINKS), 0
            for tt in range(2):
                n = 2 * i + tt
                one = lambda x: x.rearrange("p (a t) -> p a t", a=1)
                dve.wait_ge(swap_done, n + 2)
                link(dve.tensor_tensor(QT[tt][:, :], PTT[tt][:, 0:T], SIN[:, :], ALU.mult))
                link(dve.tensor_tensor(one(QS[tt][:, :]), QR[:, bass.ds(n, 1), :], one(COS[:, :]), ALU.mult))
                dve.tensor_tensor(QS[tt][:, :], QS[tt][:, :], QT[tt][:, :], ALU.add).then_inc(roped, 1)
                dve.wait_ge(sco_done, n + 1)
                ps = PTT[tt][:, :].rearrange("p (w k) -> p w k", w=NC)
                snk = SNK[:, bass.ds(n, 1)]
                dve.tensor_reduce(MX[tt][:, 0:1], ps[:, 0:1, 64:P], AX.X, ALU.max)
                link(dve.tensor_reduce(MX[tt][:, 1:4], ps[:, 1:4, :], AX.X, ALU.max))
                link(dve.tensor_scalar(MX[tt][:, :], MX[tt][:, :], ATT_SCALE, snk, ALU.mult, ALU.max))
                dve.tensor_scalar(ES[tt][:, :], MX[tt][:, :], -1.0, snk, ALU.mult, ALU.add)
                dve.tensor_scalar(NM[tt][:, :], MX[tt][:, :], -1.0, None, ALU.mult).then_inc(max_ready, 1)
                dve.wait_ge(prob_ready, n + 1)
                link(dve.tensor_tensor(DEN[tt][:, :], SU[tt][:, :], ES[tt][:, :], ALU.add))
                link(dve.reciprocal(DEN[tt][:, :], DEN[tt][:, :]))
                dve.tensor_scalar(PR[tt][:, 0, 64:P], PR[tt][:, 0, 64:P], DEN[tt][:, 0:1], None, ALU.mult)
                dve.tensor_tensor(PR[tt][:, 1:4, :], PR[tt][:, 1:4, :],
                                  DEN[tt][:, 1:4].unsqueeze(2).to_broadcast([P, 3, P]), ALU.mult).then_inc(norm_ready, 1)
                dve.wait_ge(mh_ready, 76 + n + 1)
                dve.tensor_tensor(ML[:, bass.ds(n, 1), :], PG[tt][:, 512:768].rearrange("p (a t) -> p a t", a=1),
                                  MH[:, bass.ds(n, 1), :].bitcast(F32), ALU.subtract).then_inc(ml_ready, 1)
                dve.wait_ge(ml_ready, 76 + n + 1)
            assert step.k == 2 * ATT_LINKS, step.k
        step.v = base_step + (KT // 2) * 2 * ATT_LINKS
        st = stages["ao"]
        for g in range(4):
            produce(st, g, CARRY["ao"] + g // 2, g % 2 == 1)
            if g % 2:
                ada_finish(CARRY["ao"] + g // 2)
        residual(5, "g_m1", "g11", 8, 22)
        gains("sc_f1", "g12", 26)
        inverse_rms(6)
        modulated(64, 92, "sh_f1")
        ffn(1)
        residual(7, "g_f1", "g13", 12, 28)

    ctx.close()


_INS = ["x", "c", "positions", "ada_w", "ada_b", "norm_g", "rwkv_mu", "rwkv_w_r", "rwkv_w_k", "rwkv_w_v",
        "rwkv_w0", "rwkv_w1", "rwkv_w2", "rwkv_a0", "rwkv_a1", "rwkv_a2", "rwkv_g1", "rwkv_g2", "rwkv_k_k",
        "rwkv_k_a", "rwkv_r_k", "rwkv_gn_g", "rwkv_gn_b", "rwkv_w_o", "kv_ada_w", "kv_ada_b", "kv_norm_g", "w_kv",
        "attn_w_q", "attn_sinks", "attn_w_o", "ffn_w_gu", "ffn_w_down"]


def kernel(**inputs):
    from concourse import bacc
    from concourse.bass_utils import run_bass_kernel_spmd

    nc = bacc.Bacc("TRN2", target_bir_lowering=False, num_devices=1)
    consts, at = constants()
    arrays = {"cst": consts}
    for name in _INS:
        arrays[name] = np.ascontiguousarray(inputs[name])
    args = {name: nc.dram_tensor(name, x.shape, mybir.dt.from_np(x.dtype), kind="ExternalInput").ap()
            for name, x in arrays.items()}
    out = nc.dram_tensor("out", (1, T, D), F32, kind="ExternalOutput").ap()
    trunk(nc, args, at, out)
    r = run_bass_kernel_spmd(nc, [arrays], core_ids=[0])
    return r.results[0]["out"]
```

```python
from contextlib import ExitStack

import numpy as np
import concourse.bass as bass
from concourse import mybir
from concourse.alu_op_type import AluOpType as ALU

F32 = mybir.dt.float32
F32R = mybir.dt.float32r
I32 = mybir.dt.int32
ACT = mybir.ActivationFunctionType
AX = mybir.AxisListType

P = 128
D = 2048
T = 256
KT = D // P
DFF = 5632
HT = DFF // P
C = 64
NC = T // C
LORA = 96
GLORA = 256
W_SCALE = float(np.exp(-0.5))
RMS_EPS = 1e-6
GN_EPS = 64e-5
ATT_SCALE = 64 ** -0.5
LEVELS = [2, 4, 8, 16, 32]
WARM_UP = 16
SCAN_LINKS = 9
ATT_LINKS = 6
UNITS = 28
U_KV, U_1 = 12, 16
TWO_PI_HI = 6.28125
TWO_PI_LO = float(np.float32(2 * np.pi - 6.28125))
MAGIC = 1.5 * 2.0 ** 23


def constants():
    parts, at, n = [], {}, 0

    def put(name, a):
        nonlocal n
        at[name] = (n, n + a.shape[1])
        n += a.shape[1]
        parts.append(np.asarray(a, np.float32))

    p = np.arange(P)
    e, s = p // 64, p % 64
    t = np.arange(64)
    put("ident", np.eye(P))
    put("head_ones", (e[:, None] == e[None, :]) * 1.0)
    put("stacked_ident", (s[:, None] == t[None, :]) * 1.0)
    rot = np.where(s < 8, p + 8, np.where(s < 16, p - 8, p))
    swap = np.zeros((P, P))
    swap[rot[s < 16], p[s < 16]] = 1.0
    put("rope_swap", swap)
    for half in range(2):
        put(f"dup{half}", (p[:, None] == (64 * half + s)[None, :]) * 1.0)
    put("strict", (t[None, :] > s[:, None]) * 1.0)
    put("incl", (t[None, :] >= s[:, None]) * 1.0)
    low = lambda r, c, m: ((r // m) % 2 == 1) & (c // m == r // m - 1)
    put("upper1", low(t[None, :], s[:, None], 1) * 1.0)
    for m in [1] + LEVELS:
        put(f"lower{m}", low(s[:, None], t[None, :], m) * 1.0)
    put("carry", np.broadcast_to((np.arange(T) % C != 0) * 1.0, (P, T)))
    freq = np.float32(500000.0) ** (-np.arange(0, 16, 2, dtype=np.float32) / np.float32(16))
    put("freq", np.where(s < 16, freq[s % 8], 0.0)[:, None])
    put("rope_sign", np.where(s < 8, -1.0, np.where(s < 16, 1.0, 0.0))[:, None])
    put("rms_eps", np.full((P, 1), RMS_EPS))
    return np.ascontiguousarray(np.concatenate(parts, 1)), at


PARTS = [(8, 4), (8, 4), (6, 3)]


def plan():
    order = [("r", 4, 4), ("k", 4, 4), ("v", 4, 4), ("o", 4, 4)]
    for n, (g, q) in enumerate(PARTS):
        order += [(f"gu0{n}", g, 4), (f"down0{n}", 4, q)]
    order += [("kv", 1, 4), ("q", 4, 4), ("ao", 4, 4)]
    for n, (g, q) in enumerate(PARTS):
        order += [(f"gu1{n}", g, 4), (f"down1{n}", 4, q)]
    stages, panel, group = {}, 0, 12
    for name, g, q in order:
        stages[name] = dict(name=name, groups=g, q=q, p0=panel, g0=group)
        panel += g * q
        group += g
    return stages, panel


CARRY = {"gu00": 12, "gu01": 16, "gu02": 20, "kv": 23, "q": 24, "ao": 26}


def trunk(nc, a, at, out):
    stages, PANELS = plan()
    names = list(stages)

    def after(name):
        k = names.index(name) + 1
        return stages[names[k]] if k < len(names) else None

    ctx = ExitStack()
    base = 16512
    here = [base]

    def sb(name, shape, dt=F32, offset=None):
        size = int(np.prod(shape[1:])) * 4
        if offset is None:
            offset = here[0]
            here[0] += (size + 31) // 32 * 32
        return nc.alloc_sbuf_tensor_at(name, shape, dt, offset=offset)

    def sem(name):
        return ctx.enter_context(nc.semaphore(name))

    X = sb("X", [P, KT, T])
    mh_at = here[0]
    MH = sb("MH", [P, KT, T], F32R)
    ML = sb("ML", [P, KT, T], F32R)
    RAW = [sb(f"RAW{n}", [P, 4, 512]) for n in range(4)]
    wh_at = here[0]
    WH = [sb(f"WH{n}", [P, 4, 512], F32R) for n in range(2)]
    WL = [sb(f"WL{n}", [P, 4, 512], F32R) for n in range(2)]
    ADA = [sb(f"ADA{n}", [P, 1024]) for n in range(4)]
    ACC = sb("ACC", [P, 1024])
    ncst = max(b for _, b in at.values())
    CST = sb("CST", [P, ncst])
    PM = sb("PM", [P, 640])
    MODS = sb("MODS", [P, UNITS * 8])
    CA = sb("CA", [P, KT])
    ONES = sb("ONES", [P, P])
    ONESB = sb("ONESB", [P, P], mybir.dt.bfloat16)
    WARMB = sb("WARMB", [P, 256], mybir.dt.bfloat16)
    RS = sb("RS", [P, T])
    RT = sb("RT", [P, T])
    SV = sb("SV", [P, KT])
    GG = sb("GG", [P, KT])
    OMK = sb("OMK", [P, KT])
    arena = here[0]
    K = 1024
    H = sb("H", [P, KT, T], offset=arena)
    XX = sb("XX", [P, KT, T], offset=arena + 16 * K)
    MIX = sb("MIX", [P, KT, T], offset=arena + 32 * K)
    ST = [sb(f"ST{n}", [P, 4, T], offset=arena + (48 + 4 * n) * K) for n in range(2)]
    XIN = sb("XIN", [P, 2, D], offset=arena + 32 * K)
    PROW = sb("PROW", [P, 5, P], offset=arena + 48 * K)
    TW = sb("TW", [LORA, T], offset=arena + 56 * K)
    AW = sb("AW", [LORA, T], offset=arena + 57 * K)
    GW = sb("GW", [P, 2, T], offset=arena + 58 * K)
    Y = sb("Y", [P, KT, T], offset=arena)
    HH = sb("HH", [P, 16, T], F32R, offset=arena + 16 * K)
    HL = sb("HL", [P, 16, T], F32R, offset=arena + 32 * K)
    SQ = [sb(f"SQ{n}", [P, 4, T], offset=arena + (48 + 4 * n) * K) for n in range(2)]
    SG = [sb(f"SG{n}", [P, 2, T], offset=arena + (48 + 2 * n) * K) for n in range(2)]
    HID = [sb(f"HID{n}", [P, 2, T], offset=arena + (52 + 2 * n) * K) for n in range(2)]
    top = [arena]

    def sc(name, *shape):
        size = (int(np.prod(shape)) * 4 + 31) // 32 * 32
        top[0] += size
        return sb(name, [P, *shape], offset=top[0] - size)

    IN = [sc(f"IN{n}", 5, T) for n in range(2)]
    KSQ, NRM, KK, CUM, CME, WI, WV, WE, T1, KP, RR, KKA, KW = (sc(n, T) for n in (
        "KSQ", "NRM", "KK", "CUM", "CME", "WI", "WV", "WE", "T1", "KP", "RR", "KKA", "KW"))
    AR = [sc(f"AR{n}", NC, 2, C) for n in range(2)]
    BST = sc("BST", NC, C)
    YC, YQ = sc("YC", NC, C), sc("YQ", NC, C)
    YN = sc("YN", NC, C)
    Y2 = sc("Y2", T)
    SS = [sc(f"SS{n}", C) for n in range(2)]
    SW, RH, UU = sc("SW", C), sc("RH", C), sc("UU", C)
    MS, VS, VR, HALF = sc("MS", NC), sc("VS", NC), sc("VR", NC), sc("HALF", NC)
    WCA = sc("WCA", KT, NC)
    scan_top = top[0]
    top[0] = wh_at
    TOKV = [sc(f"TOKV{n}", NC, C) for n in range(2)]
    TOKBK = [sc(f"TOKBK{n}", 2, NC, C) for n in range(2)]
    ARB, AAK, ARK, NI = ([sc(f"{x}{n}", NC, C) for n in range(2)] for x in ("ARB", "AAK", "ARK", "NI"))
    AM = [sc(f"AM{n}", NC, C) for n in range(2)]
    AST = sc("AST", NC, C)
    NT = sc("NT", NC, 2, C)
    PC = sc("PC", NC, C)
    assert top[0] <= wh_at + 32 * K
    BV = sb("BV", [P, KT, T], offset=mh_at)
    GATE = sb("GATE", [P, KT, T], offset=mh_at + 16 * K)
    top[0] = arena + 16 * K
    QR = Y
    KR, VR2, KX = sc("KR", 2, T), sc("VTR", 2, T), sc("KX", 2, T)
    KD, VW = sc("KD", 4, T), sc("VW", NC, T)
    QS = [sc(f"QS{n}", T) for n in range(2)]
    QT = [sc(f"QT{n}", T) for n in range(2)]
    PR = [sc(f"PR{n}", NC, P) for n in range(2)]
    PT = [sc(f"PT{n}", NC, P) for n in range(2)]
    COS, SIN, ANG, TURN = sc("COS", T), sc("SIN", T), sc("ANG", T), sc("TURN", T)
    assert top[0] <= arena + 48 * K
    top[0] = arena + 56 * K
    SNK, SNKA = sc("SNK", KT), sc("SNKA", 2 * KT)
    MX, NM, SU, ES, DEN = ([sc(f"{n}{m}", NC) for m in range(2)] for n in ("MX", "NM", "SU", "ES", "DEN"))
    POSI = sb("POSI", [P, T], I32, offset=arena + 57 * K)
    XO = sb("XO", [P, 2, D], offset=arena + 16 * K)
    assert scan_top <= 229344 and arena + 60 * K <= 229344, (scan_top, arena)

    PG = [nc.alloc_psum_tensor(f"PG{n}", [P, 1024], F32) for n in range(2)]
    PS = nc.alloc_psum_tensor("PS", [P, 512], F32)
    PA = nc.alloc_psum_tensor("PA", [P, 512], F32)
    PT0 = nc.alloc_psum_tensor("PT0", [P, 512], F32)
    PT1 = nc.alloc_psum_tensor("PT1", [P, 512], F32)
    PTT = [PT0, PT1]

    SCR = nc.dram_tensor("scan_inputs", [KT, P, 6, T], F32, kind="Internal").ap()

    cst = lambda name: CST[:, at[name][0]:at[name][1]]
    col = {}
    for l in range(2):
        for i in range(4):
            col[f"g{l}{i}"] = (4 * l + i) * 16
    col["bias"] = 128
    col["kvg"], col["c"] = 352, 368
    for i in range(6):
        col[f"mu{i}"] = 384 + 16 * i
    col["w0"], col["a0"] = 480, 496
    for n, name in enumerate(["k_k", "k_a", "r_k", "gn_g", "gn_b"]):
        col[name] = 512 + 16 * n
    pm = lambda name: PM[:, col[name]:col[name] + 16]
    MOD = {}
    for l, u in ((0, 0), (1, U_1)):
        for i, name in enumerate(["sh_m", "sc_m", "g_m", "sh_f", "sc_f", "g_f"]):
            MOD[f"{name}{l}"] = 8 * u + 16 * i
    MOD["sh_kv"], MOD["sc_kv"] = 8 * U_KV, 8 * U_KV + 16
    mod = lambda name: MODS[:, MOD[name]:MOD[name] + 16]

    cst_full, par_full, x_full = sem("cst_full"), sem("par_full"), sem("x_full")
    raw_full = [sem(f"raw_full{n}") for n in range(4)]
    lora_full = [sem(f"lora_full{n}") for n in range(4)]
    ada_full = [sem(f"ada_full{n}") for n in range(4)]
    in_full = [sem(f"in_full{n}") for n in range(2)]
    scr_stored = [sem(f"scr_stored{n}") for n in range(2)]
    out_stored, att_full = sem("out_stored"), sem("att_full")
    wh_ready, wl_ready, wlp_ready = sem("wh_ready"), sem("wl_ready"), sem("wlp_ready")
    panel_used = sem("panel_used")
    mh_ready, ml_ready = sem("mh_ready"), sem("ml_ready")
    hh_ready, hl_ready, sg_ready, hid_ready = sem("hh_ready"), sem("hl_ready"), sem("sg_ready"), sem("hid_ready")
    ada_used, red_done, mods_ready = sem("ada_used"), sem("red_done"), sem("mods_ready")
    ones_set, par_turned, par_copied, ca_ready = sem("ones_set"), sem("par_turned"), sem("par_copied"), sem("ca_ready")
    x_turned, x_copied = sem("x_turned"), sem("x_copied")
    squared, sq_used, rt_ready, rs_ready = sem("squared"), sem("sq_used"), sem("rt_ready"), sem("rs_ready")
    scaled, h_ready, mix_ready, mix_used, mix_full = sem("scaled"), sem("h_ready"), sem("mix_ready"), sem("mix_used"), sem("mix_full")
    lora_mid, lora_done = sem("lora_mid"), sem("lora_done")
    st_ready, y_ready, x_ready, v_step = sem("st_ready"), sem("y_ready"), sem("x_ready"), sem("v_step")
    (ksq_ready, ss_done, nrm_ready, cum_ready, cme_ready, exp_ready, t1_ready, kp_ready, rr_ready,
     bonus_done, bv_ready, kk_ready, kka_ready, ar_ready, b_ready, kw_ready, pb_done, ast_done, pk_done,
     tok_done, ast_ready, tokv_ready, tok_ready, coef_ready, nt_ready, am_ready, p_done, p_copied, d_done,
     ni_ready, rhs_done, rhs_ready, u_done, u_ready, sd_done, s_ready, y_done, yc_ready, yq_ready, vs_ready,
     vr_ready, yn_ready, yt_done, yt_read, yo_ready, half_set, g_full) = (sem(n) for n in (
         "ksq_ready ss_done nrm_ready cum_ready cme_ready exp_ready t1_ready kp_ready rr_ready "
         "bonus_done bv_ready kk_ready kka_ready ar_ready b_ready kw_ready pb_done ast_done pk_done "
         "tok_done ast_ready tokv_ready tok_ready coef_ready nt_ready am_ready p_done p_copied d_done "
         "ni_ready rhs_done rhs_ready u_done u_ready sd_done s_ready y_done yc_ready yq_ready vs_ready "
         "vr_ready yn_ready yt_done yt_read yo_ready half_set g_full").split())
    (kv_copied, q_copied, rope_ready, swap_done, roped, kd_done, kd_ready, vw_done, vw_ready, sco_done, max_ready,
     prob_ready, es_ready, norm_ready, pt_done, pt_ready, o_done, turned, drained, sin_ready) = (sem(n) for n in (
         "kv_copied q_copied rope_ready swap_done roped kd_done kd_ready vw_done vw_ready sco_done max_ready "
         "prob_ready es_ready norm_ready pt_done pt_ready o_done turned drained sin_ready").split())

    block = ctx.enter_context(nc.Block())

    class Tally:
        def __init__(self, semaphore, value=0):
            self.sem, self.v, self.k = semaphore, value, 0

        def add(self, ins):
            ins.then_inc(self.sem, 1)
            self.v, self.k = self.v + 1, self.k + 1
            return self.v

    gu = [a["ffn_w_gu"][l].rearrange("(k p) (h n) -> p k h n", p=P, h=2) for l in range(2)]
    down = [a["ffn_w_down"][l].rearrange("(k p) n -> p k n", p=P) for l in range(2)]
    square = {"r": a["rwkv_w_r"][0], "k": a["rwkv_w_k"][0], "v": a["rwkv_w_v"][0], "o": a["rwkv_w_o"][0],
              "kv": a["w_kv"], "q": a["attn_w_q"][0], "ao": a["attn_w_o"][0]}
    square = {n: w.rearrange("(k p) n -> p k n", p=P) for n, w in square.items()}

    def halves(st, g, q):
        name, slot = st["name"], (st["p0"] + (g * st["q"] if isinstance(g, int) else 0) + q) % 4
        raw = RAW[slot]
        if name.startswith("gu"):
            g_all = g + sum(x for x, _ in PARTS[:int(name[3])])
            w = gu[int(name[2])]
            return slot, [(raw[:, :, 256 * h:256 * h + 256], w[:, 4 * q:4 * q + 4, h, bass.ds(g_all * 256, 256)])
                          for h in range(2)]
        if name.startswith("down"):
            k0 = 16 * int(name[5]) + 4 * q
            w = down[int(name[4])]
        else:
            k0, w = 4 * q, square[name]
        return slot, [(raw[:, 2 * h:2 * h + 2, :], w[:, k0 + 2 * h:k0 + 2 * h + 2, bass.ds(g * 512, 512)])
                      for h in range(2)]

    ada = [a["ada_w"][l].rearrange("(k p) n -> k p n", p=P) for l in range(2)]
    kva = a["kv_ada_w"].rearrange("(k p) n -> k p n", p=P)

    def ada_source(first, u, step):
        w, c0 = (ada[0], 0) if first < U_KV else (kva, U_KV) if first < U_1 else (ada[1], U_1)
        return w[step][:, bass.ds((first - c0 + u) * 1024, 1024)]

    @block.sync
    def _(sp):
        def ada_load(first, u, step):
            n = 16 * (first + u) + step
            if not (isinstance(n, int) and n < 4):
                sp.wait_ge(ada_used, n - 3)
            sp.dma_start(ADA[step % 4][:, :], ada_source(first, u, step)).then_inc(ada_full[step % 4], 16)

        def panel_load(st, g, q):
            n = st["p0"] + g * st["q"] + q
            slot, parts = halves(st, g, q)
            if isinstance(n, int) and n < 4:
                sp.wait_ge(lora_done, [4, 8, 12, 12][n])
            else:
                sp.wait_ge(wl_ready, n - 3)
                sp.wait_ge(wlp_ready, n - 3)
            for dst, src in parts:
                sp.dma_start(dst, src).then_inc(raw_full[slot], 16)

        def stage_loads(st):
            name, n = st["name"], st["groups"]
            first = CARRY.get(name)
            nxt = after(name)

            def body(g, u, odd, target, tg):
                for q in range(4):
                    if first is not None:
                        for s in range(4 if name == "kv" else 2):
                            ada_load(first, u, (4 if name == "kv" else 2) * q + s + (8 if odd else 0))
                    if target is not None and q < target["q"]:
                        panel_load(target, tg, q)

            if n > 4:
                with sp.Fori(0, n // 2 - 1) as i:
                    body(2 * i, i, False, st, 2 * i + 1)
                    body(2 * i + 1, i, True, st, 2 * i + 2)
                body(n - 2, n // 2 - 1, False, st, n - 1)
            else:
                for g in range(n - 1):
                    body(g, g // 2, g % 2 == 1, st, g + 1)
            body(n - 1, (n - 1) // 2, n > 1, nxt, 0)

        sp.dma_start(CST[:, :], a["cst"]).then_inc(cst_full, 16)
        for u in range(2):
            for s in range(16):
                ada_load(u, 0, s)
        sp.dma_start(XIN[:, :, :], a["x"][0].rearrange("(h p) d -> p h d", p=P)).then_inc(x_full, 16)
        for u in range(2, 4):
            for s in range(16):
                ada_load(u, 0, s)
        lora_tile = lambda n, w: RAW[n][:, :, :].rearrange("p a b -> p (a b)")[:, 0:w]
        for n, name in enumerate(["rwkv_w1", "rwkv_a1"]):
            sp.dma_start(lora_tile(n, KT * LORA).rearrange("p (k n) -> p k n", k=KT),
                         a[name][0].rearrange("(k p) n -> p k n", p=P)).then_inc(lora_full[n], 16)
        g1 = a["rwkv_g1"][0].rearrange("(k p) n -> p k n", p=P)
        for n in range(2):
            sp.dma_start(RAW[2 + n][:, :, :].rearrange("p a (b n) -> p (a b) n", b=2),
                         g1[:, 8 * n:8 * n + 8, :]).then_inc(lora_full[2 + n], 16)
        for n, name in enumerate(["rwkv_w2", "rwkv_a2"]):
            sp.wait_ge(mix_used, KT * (n + 1))
            sp.dma_start(RAW[n][0:LORA, :, :].rearrange("p a b -> p (a b)"), a[name][0]).then_inc(lora_full[n], 16)
        sp.wait_ge(mix_used, 3 * KT)
        for n in range(2):
            sp.dma_start(RAW[2 + n][:, :, :].rearrange("p a b -> p (a b)"),
                         a["rwkv_g2"][0][P * n:P * n + P, :]).then_inc(lora_full[2 + n], 16)
        for q in range(4):
            panel_load(stages["r"], 0, q)
        for name in ("r", "k"):
            stage_loads(stages[name])
        for g in range(1, 4):
            for q in range(4):
                panel_load(stages["v"], g, q)
        for q in range(4):
            panel_load(stages["o"], 0, q)
        for stores in scr_stored:
            sp.wait_ge(stores, 16 * 12)
        for n in range(2):
            sp.dma_start(IN[n][:, :, :], SCR[n, :, 0:5, :]).then_inc(in_full[n], 16)
        sp.wait_ge(panel_used, 48)
        sp.dma_start(GATE[:, :, :], SCR[:, :, 5, :].rearrange("k p t -> p k t")).then_inc(g_full, 16)

        def scan_load(n, par):
            sp.wait_ge(tok_done, n - 1)
            sp.wait_ge(bv_ready, n - 1)
            sp.dma_start(IN[par][:, :, :], SCR[bass.ds(n, 1), :, 0:5, :].rearrange("a p q t -> p (a q) t"))\
              .then_inc(in_full[par], 16)

        scan_load(2, 0)
        for s in range(4):
            ada_load(4, 0, s)

        def scan_loads(i, tt, load):
            if load:
                scan_load(2 * i + tt + 3, (tt + 1) % 2)
            for s in range(8):
                if tt == 0 or s < 4:
                    ada_load(4, i, 8 * tt + 4 + s)
                elif not isinstance(i, int) or i < 7:
                    ada_load(4, i + 1, s - 4)

        with sp.Fori(0, 6) as i:
            for tt in range(2):
                scan_loads(i, tt, True)
        for n in range(12, KT):
            scan_loads(n // 2, n % 2, n == 12)
        for name in names[names.index("o"):]:
            if name == "q":
                sp.dma_start(SNKA[:, :], a["attn_sinks"].to_broadcast([P, 2 * KT])).then_inc(att_full, 16)
                sp.dma_start(POSI[:, :], a["positions"][0:1, :].to_broadcast([P, T])).then_inc(att_full, 16)
            stage_loads(stages[name])
        sp.wait_ge(drained, 8)
        sp.dma_start(out[0].rearrange("(h p) d -> p h d", p=P), XO[:, :, :]).then_inc(out_stored, 16)
        sp.wait_ge(out_stored, 16)

    @block.gpsimd
    def _(pool):
        def residue(n, q):
            pool.wait_ge(wh_ready, n + 1)
            if not (isinstance(n, int) and n < 2):
                pool.wait_ge(panel_used, n - 1)
            pool.tensor_tensor(WL[q % 2][:, 2:4, :], RAW[q][:, 2:4, :], WH[q % 2][:, 2:4, :].bitcast(F32),
                               ALU.subtract).then_inc(wlp_ready, 1)

        pool.memset(ONES[:, :], 1.0).then_inc(ones_set, 1)
        pool.memset(WARMB[:, :], 1.0).then_inc(ones_set, 1)
        pool.memset(ONESB[:, :], 1.0).then_inc(ones_set, 1)
        for n in range(4):
            residue(n, n)
        with pool.Fori(1, 12) as i:
            for q in range(4):
                residue(4 * i + q, q)
        for stores in scr_stored:
            pool.wait_ge(stores, 16 * 12)
        pool.wait_ge(panel_used, 48)
        pool.memset(HALF[:, :], -0.5).then_inc(half_set, 1)
        pool.wait_ge(half_set, 1)

        def scan_body(n, k):
            x = IN[k % 2]

            def level_entries(lv):
                if not 0 <= k + 1 < KT:
                    return
                if lv >= 2:
                    pool.wait_ge(p_done, 10 * n + 2 * lv + 8)
                elif k >= 0:
                    pool.wait_ge(p_done, 10 * n + 8 + 2 * lv)
                pool.tensor_tensor(AM[lv % 2][:, :, :], AST[:, :, :],
                                   cst(f"lower{LEVELS[lv]}").unsqueeze(1).to_broadcast([P, NC, C]), ALU.mult)\
                    .then_inc(am_ready, 1)

            if 0 <= k + 1 < KT:
                pool.wait_ge(ast_ready, n + 2)
            level_entries(0)
            level_entries(1)
            if k + 2 < KT:
                pool.wait_ge(cum_ready, n + 3)
                if k + 2 >= 1:
                    pool.wait_ge(exp_ready, n + 2)
                pool.tensor_tensor(CME[:, :], CUM[:, :], x[:, 4, :], ALU.subtract).then_inc(cme_ready, 1)
                pool.wait_ge(t1_ready, n + 3)
                if k + 2 >= 1:
                    pool.wait_ge(rr_ready, n + 2)
                pool.tensor_tensor(KP[:, :], x[:, 1, :], T1[:, :], ALU.mult).then_inc(kp_ready, 1)
            level_entries(2)
            level_entries(3)
            if 0 <= k - 1 < KT:
                pool.wait_ge(vs_ready, n)
                pool.tensor_tensor(VR[:, :], VS[:, :], HALF[:, :], ALU.pow).then_inc(vr_ready, 1)
            level_entries(4)
            if k + 2 < KT:
                pool.wait_ge(kk_ready, n + 3)
                pool.tensor_tensor(KKA[:, :], KK[:, :], x[:, 3, :], ALU.mult).then_inc(kka_ready, 1)
                pool.wait_ge(exp_ready, n + 3)
                pool.wait_ge(kp_ready, n + 3)
                if k + 1 >= 0:
                    pool.wait_ge(pk_done, n + 2)
                pool.tensor_tensor(KW[:, :], KP[:, :], WV[:, :], ALU.mult).then_inc(kw_ready, 1)

        for n in range(-2, 2):
            scan_body(n, n)
        with pool.Fori(0, 6) as i:
            for tt in range(2):
                scan_body(2 * i + 2 + tt, 2 + tt)
        for n in range(14, 18):
            scan_body(n, n)
        pool.wait_ge(ml_ready, 12 + KT)
        for q in range(4):
            residue(48 + q, q)
        with pool.Fori(13, PANELS // 4) as i:
            for q in range(4):
                residue(4 * i + q, q)

    @block.scalar
    def _(act):
        def rounded(n, slot=None, full=None):
            if isinstance(n, int):
                slot, full = n % 4, 32 * (n // 4) + 32
            act.wait_ge(raw_full[slot], full)
            if not (isinstance(n, int) and n < 2):
                act.wait_ge(panel_used, n - 1)
            act.activation(WH[slot % 2][:, :, :], RAW[slot][:, :, :], ACT.Copy).then_inc(wh_ready, 1)

        stored = [0]

        def to_scratch(gi, tiles, quantity, make, wait):
            k = stored[0]
            act.wait_ge(*wait)
            if k >= 2:
                act.wait_ge(scr_stored[k % 2], 16 * (k // 2))
            make(ST[k % 2], PG[gi % 2])
            act.wait_ge(st_ready, k + 1)
            act.dma_start(SCR[tiles:tiles + 4, :, quantity, :].rearrange("j p n -> p j n"), ST[k % 2][:, :, :])\
               .then_inc(scr_stored[k % 2], 16)
            stored[0] += 1

        def rooted(n):
            act.wait_ge(sq_used, 4 * n + 4)
            if n:
                act.wait_ge(rs_ready, n)
            act.activation(RT[:, :], PS[:, 0:T], ACT.Sqrt, bias=cst("rms_eps"), scale=1.0 / D).then_inc(rt_ready, 1)

        nsq = [0]

        def squares(src, ready):
            for q in range(4):
                act.wait_ge(*ready(q))
                if nsq[0] >= 2:
                    act.wait_ge(sq_used, nsq[0] - 1)
                act.activation(SQ[nsq[0] % 2][:, :, :], src[:, 4 * q:4 * q + 4, :], ACT.Square).then_inc(squared, 1)
                nsq[0] += 1

        def shifted(nh, shift, free):
            for k in range(KT):
                act.wait_ge(scaled, nh + k + 1)
                if k % 4 == 0 and free is not None:
                    act.wait_ge(panel_used, free + k // 4 + 1)
                act.activation(MH[:, k, :], Y[:, k, :], ACT.Identity, bias=mod(shift)[:, k:k + 1]).then_inc(mh_ready, 1)

        rows = [(0, 0, a["norm_g"].rearrange("l i (k n) -> (l i k) n", n=P)),
                (1, 0, a["ada_b"][0:1].rearrange("a (k n) -> (a k) n", n=P)),
                (1, 96, a["kv_ada_b"].rearrange("(k n) -> k n", n=P)),
                (2, 0, a["ada_b"][1:2].rearrange("a (k n) -> (a k) n", n=P)),
                (2, 96, a["kv_norm_g"].rearrange("(k n) -> k n", n=P)),
                (2, 112, a["c"].rearrange("a (k n) -> (a k) n", n=P)),
                (3, 0, a["rwkv_mu"][0].rearrange("i (k n) -> (i k) n", n=P)),
                (3, 96, a["rwkv_w0"].rearrange("a (k n) -> (a k) n", n=P)),
                (3, 112, a["rwkv_a0"].rearrange("a (k n) -> (a k) n", n=P)),
                (4, 0, a["rwkv_k_k"].rearrange("a (k n) -> (a k) n", n=P)),
                (4, 16, a["rwkv_k_a"].rearrange("a (k n) -> (a k) n", n=P)),
                (4, 32, a["rwkv_r_k"][0].rearrange("(k e) n -> k (e n)", e=2)),
                (4, 48, a["rwkv_gn_g"].rearrange("a (k n) -> (a k) n", n=P)),
                (4, 64, a["rwkv_gn_b"].rearrange("a (k n) -> (a k) n", n=P))]
        for b, r, src in rows:
            act.dma_start(PROW[r:r + src.shape[0], b, :], src).then_inc(par_full, 16)
        act.wait_ge(par_turned, 1)
        act.activation(PM[:, 0:592], PG[0][:, 0:592], ACT.Copy).then_inc(par_copied, 1)
        act.wait_ge(par_copied, 1)
        act.activation(CA[:, :], pm("c"), ACT.Silu).then_inc(ca_ready, 1)
        for g in range(4):
            act.wait_ge(x_turned, g + 1)
            act.activation(X[:, 4 * g:4 * g + 4, :], PG[g % 2][:, :].rearrange("p (j t) -> p j t", j=4),
                           ACT.Copy).then_inc(x_copied, 1)
        squares(X, lambda q: (x_copied, 4))
        rooted(0)
        for k in range(KT):
            act.wait_ge(scaled, k + 1)
            act.activation(H[:, k, :], MIX[:, k, :], ACT.Identity, bias=mod("sh_m0")[:, k:k + 1]).then_inc(h_ready, 1)
        def lora_group(L, g, quantity, bias, done):
            def make(dst, src):
                for j in range(4):
                    ins = act.activation(dst[:, j, :], src[:, T * j:T * j + T], ACT.Sigmoid,
                                         bias=pm(bias)[:, 4 * g + j:4 * g + j + 1])
                ins.then_inc(st_ready, 1)
            to_scratch(L, 4 * g, quantity, make, (lora_done, done))

        def plain(dst, src):
            act.activation(dst[:, :, :], src[:, :].rearrange("p (j t) -> p j t", j=4), ACT.Copy).then_inc(st_ready, 1)

        act.wait_ge(mix_used, KT)
        act.activation(TW[:, :], PT0[0:LORA, 0:T], ACT.Tanh).then_inc(lora_mid, 1)
        act.wait_ge(mix_used, 2 * KT)
        act.activation(AW[:, :], PT1[0:LORA, 0:T], ACT.Copy).then_inc(lora_mid, 1)
        for g in range(4):
            lora_group(g, g, 4, "w0", g + 1)
        act.wait_ge(mix_used, 3 * KT)
        act.activation(GW[:, :, :], PT0[:, :].rearrange("p (j t) -> p j t", j=2), ACT.Sigmoid).then_inc(lora_mid, 1)
        for g in range(4):
            lora_group(4 + g, g, 3, "a0", 5 + g)
        for g in range(4):
            to_scratch(8 + g, 4 * g, 5, plain, (lora_done, 9 + g))
        rounded(0)

        def mix_rounded(nm):
            q = nm % 4
            act.wait_ge(mix_full, nm + 1)
            if nm >= 4:
                act.wait_ge(panel_used, 16 * (nm // 4) - 4 + q + 1)
            act.activation(MH[:, 4 * q:4 * q + 4, :], MIX[:, 4 * q:4 * q + 4, :], ACT.Copy).then_inc(mh_ready, 1)

        for q in range(4):
            mix_rounded(q)
        for s, name in enumerate(("r", "k", "v")):
            st = stages[name]
            for g in range(4):
                for q in range(4):
                    if st["p0"] + 4 * g + q + 1 < 48:
                        rounded(st["p0"] + 4 * g + q + 1)
                    if g == 3 and q >= 1 and s < 2:
                        mix_rounded(4 * (s + 1) + q - 1)
                to_scratch(st["g0"] + g, 4 * g, s, plain, (panel_used, st["p0"] + 4 * g + 4))
            if s < 2:
                mix_rounded(4 * (s + 1) + 3)

        for stores in scr_stored:
            act.wait_ge(stores, 16 * 12)
        c4 = lambda x: x.rearrange("p (c t) -> p c t", c=NC)

        def scan_body(n, k):
            par, nxt = k % 2, (k + 1) % 2
            prep, inverse, recur, norm = k + 2 < KT, 0 <= k + 1 < KT, 0 <= k < KT, 0 <= k - 1 < KT
            x = IN[par]

            def rhs_copy(c):
                if recur:
                    act.wait_ge(rhs_done, 4 * n + c + 1)
                    act.activation(RH[:, :], PT0[:, 0:C], ACT.Copy).then_inc(rhs_ready, 1)

            def u_copy(c):
                if recur:
                    act.wait_ge(u_done, 4 * n + c + 1)
                    act.activation(UU[:, :], PT0[:, C:2 * C], ACT.Copy).then_inc(u_ready, 1)

            def p_copy(lv):
                if inverse:
                    for hb in range(2):
                        act.wait_ge(p_done, 10 * n + 10 + 2 * lv + hb + 1)
                        act.activation(PC[:, 2 * hb:2 * hb + 2, :],
                                       PG[1][:, 512 * hb:512 * hb + 2 * C].rearrange("p (c t) -> p c t", c=2), ACT.Copy)\
                           .then_inc(p_copied, 1)

            rhs_copy(0)
            if inverse:
                act.wait_ge(ast_done, n + 2)
                if k >= 0:
                    act.wait_ge(am_ready, 5 * n + 5)
                    act.wait_ge(nt_ready, 9 * n + 1)
                act.activation(AST[:, :, :], c4(PG[1][:, 0:T]), ACT.Copy).then_inc(ast_ready, 1)
            u_copy(0)
            if inverse:
                act.activation(TOKV[nxt][:, :, :], c4(PG[1][:, T:2 * T]), ACT.Copy).then_inc(tokv_ready, 1)
                act.wait_ge(tok_done, n + 2)
                act.activation(TOKBK[nxt][:, :, :, :], PG[1][:, 2 * T:4 * T].rearrange("p (b c t) -> p b c t", b=2, c=NC),
                               ACT.Copy).then_inc(tok_ready, 1)
            if prep:
                act.wait_ge(in_full[par], 16 * ((n + 2) // 2 if isinstance(n, int) else prep_round[0]) + 16)
                act.activation(KSQ[:, :], x[:, 1, :], ACT.Square, scale=PM[:, bass.ds(col["k_k"] + n + 2, 1)])\
                   .then_inc(ksq_ready, 1)
            if norm:
                act.wait_ge(yc_ready, n)
                act.activation(YQ[:, :, :], YC[:, :, :], ACT.Square).then_inc(yq_ready, 1)
            p_copy(0)
            rhs_copy(1)
            u_copy(1)
            p_copy(1)
            rhs_copy(2)
            if prep:
                act.wait_ge(ss_done, n + 3)
                act.activation(NRM[:, :], PS[:, 0:T], ACT.Sqrt).then_inc(nrm_ready, 1)
            p_copy(2)
            u_copy(2)
            if prep:
                act.wait_ge(cum_ready, n + 3)
                act.wait_ge(cme_ready, n + 3)
                if k + 2 >= 1:
                    act.wait_ge(kw_ready, n + 2)
                    act.wait_ge(ar_ready, n + 2)
                act.activation(WI[:, :], CUM[:, :], ACT.Exp, scale=-W_SCALE)
                act.activation(WV[:, :], CUM[:, :], ACT.Exp, scale=W_SCALE)
                act.activation(WE[:, :], CME[:, :], ACT.Exp, scale=-W_SCALE).then_inc(exp_ready, 1)
            p_copy(3)
            rhs_copy(3)
            u_copy(3)
            p_copy(4)
            if norm:
                act.wait_ge(yo_ready, n)
                act.activation(MH[:, bass.ds(n - 1, 1), :], Y2[:, :].rearrange("p (a t) -> p a t", a=1), ACT.Copy)\
                   .then_inc(mh_ready, 1)

        prep_round = [0]
        for n in range(-2, 2):
            scan_body(n, n)
        with act.Fori(0, 6) as i:
            prep_round[0] = i + 2
            for tt in range(2):
                scan_body(2 * i + 2 + tt, 2 + tt)
        for n in range(14, 18):
            scan_body(n, n)
        act.wait_ge(ml_ready, 12 + KT)
        rounded(48)

        def y_evacuation(st, g, squares_too=False):
            act.wait_ge(panel_used, st["p0"] + st["q"] * (g + 1))
            act.activation(Y[:, 4 * g:4 * g + 4, :], PG[(st["g0"] + g) % 2][:, :].rearrange("p (j t) -> p j t", j=4),
                           ACT.Copy).then_inc(y_ready, 1)

        def produce(st, g):
            for q in range(st["q"]):
                n = st["p0"] + st["q"] * g + q + 1
                if not isinstance(n, int) or n < PANELS:
                    if isinstance(n, int):
                        rounded(n)
                    else:
                        slot = (st["p0"] + q + 1) % 4
                        rounded(n, slot, 8 * n + (32 - 8 * slot))

        def ffn(l):
            for part in range(3):
                st = stages[f"gu{l}{part}"]
                h0 = sum(x for x, _ in PARTS[:part])
                hall = 22 * l + h0
                with act.Fori(0, st["groups"] // 2) as i:
                    for j in range(2):
                        g = 2 * i + j
                        produce(st, g)
                        act.wait_ge(panel_used, st["p0"] + 4 * g + 4)
                        act.wait_ge(hid_ready, hall + g + 1)
                        act.activation(SG[j][:, :, :], PG[(st["g0"] + j) % 2][:, 0:512]
                                       .rearrange("p (j t) -> p j t", j=2), ACT.Silu).then_inc(sg_ready, 1)
                        act.wait_ge(hid_ready, hall + g + 3)
                        act.activation(HH[:, bass.ds(2 * g, 2), :], HID[j][:, :, :], ACT.Copy).then_inc(hh_ready, 1)
                st = stages[f"down{l}{part}"]
                for g in range(4):
                    produce(st, g)
                    if part == 0:
                        y_evacuation(st, g)

        produced = stages["o"]
        for g in range(4):
            produce(produced, g)
            y_evacuation(produced, g)
        squares(Y, lambda q: (y_ready, q + 2))
        rooted(1)
        squares(X, lambda q: (x_ready, q + 1))
        rooted(2)
        shifted(16, "sh_f0", None)
        ffn(0)
        squares(Y, lambda q: (y_ready, 17))
        rooted(3)
        squares(X, lambda q: (x_ready, 4 + q + 1))
        rooted(4)
        shifted(32, "sh_kv", None)
        st = stages["kv"]
        produce(st, 0)
        act.wait_ge(panel_used, st["p0"] + 4)
        pg = PG[st["g0"] % 2][:, :].rearrange("p (j t) -> p j t", j=4)
        act.activation(KR[:, :, :], pg[:, 0:2, :], ACT.Copy).then_inc(kv_copied, 1)
        act.activation(VR2[:, :, :], pg[:, 2:4, :], ACT.Copy).then_inc(kv_copied, 1)
        shifted(48, "sh_m1", None)
        act.wait_ge(rope_ready, 1)
        act.activation(SIN[:, :], ANG[:, :], ACT.Sin)
        act.activation(COS[:, :], ANG[:, :], ACT.Sin, scale=0.5).then_inc(sin_ready, 1)
        st = stages["q"]
        for g in range(4):
            produce(st, g)
            act.wait_ge(panel_used, st["p0"] + 4 * g + 4)
            act.activation(QR[:, 4 * g:4 * g + 4, :], PG[(st["g0"] + g) % 2][:, :].rearrange("p (j t) -> p j t", j=4),
                           ACT.Copy).then_inc(q_copied, 1)
        act.wait_ge(kd_done, 1)
        act.activation(KD[:, :, :], PG[0][:, :].rearrange("p (g t) -> p g t", g=4), ACT.Copy).then_inc(kd_ready, 1)
        act.wait_ge(vw_done, 1)
        act.activation(VW[0:64, 0, :], PG[1][0:64, 0:T], ACT.Copy)
        act.activation(VW[:, 1:4, :], PG[1][:, T:4 * T].rearrange("p (n c) -> p n c", n=3), ACT.Copy).then_inc(vw_ready, 1)
        with act.Fori(0, KT // 2) as i:
            for tt in range(2):
                n = 2 * i + tt
                act.wait_ge(max_ready, n + 1)
                for w in range(NC):
                    lo = 64 if w == 0 else 0
                    act.activation(PR[tt][:, w, lo:P], PTT[tt][:, P * w + lo:P * w + P], ACT.Exp,
                                   bias=NM[tt][:, w:w + 1], scale=ATT_SCALE, accum_out=SU[tt][:, w:w + 1])
                act.activation(ES[tt][:, :], ES[tt][:, :], ACT.Exp).then_inc(prob_ready, 1)
                act.wait_ge(pt_done, n + 1)
                pt = PG[tt][:, 0:512].rearrange("p (w q) -> p w q", w=NC)
                act.activation(PT[tt][0:64, 0, :], pt[0:64, 0, :], ACT.Copy)
                act.activation(PT[tt][:, 1:4, :], pt[:, 1:4, :], ACT.Copy).then_inc(pt_ready, 1)
                act.wait_ge(o_done, n + 1)
                act.activation(MH[:, bass.ds(n, 1), :], PG[tt][:, 512:768].rearrange("p (a t) -> p a t", a=1),
                               ACT.Copy).then_inc(mh_ready, 1)
        st = stages["ao"]
        for g in range(4):
            produce(st, g)
            y_evacuation(st, g)
        squares(Y, lambda q: (y_ready, 21))
        rooted(5)
        squares(X, lambda q: (x_ready, 8 + q + 1))
        rooted(6)
        shifted(64, "sh_f1", None)
        ffn(1)
        squares(Y, lambda q: (y_ready, 33))
        rooted(7)
        for g in range(8):
            act.wait_ge(turned, g + 1)
            act.activation(XO[:, g // 4, 512 * (g % 4):512 * (g % 4) + 512], PTT[g % 2][:, :], ACT.Copy)\
               .then_inc(drained, 1)

    @block.tensor
    def _(pe):
        mm = pe.matmul

        def take_wait(o):
            mm(o, ONESB[:, :], ONESB[:, 0:o.shape[-1]], start=True, stop=True)

        def reduce_unit(u):
            pe.wait_ge(ada_used, 16 * u + 16)
            for j in range(8):
                ins = mm(PA[:, j:j + 1], ACC[:, P * j:P * j + P], ONES[:, 0:1], start=True, stop=True)
            ins.then_inc(red_done, 1)

        def group(st, g, hi, lo, parity, moving):
            pg = PG[parity]
            for q in range(st["q"]):
                n = st["p0"] + st["q"] * g + q
                slot = (st["p0"] + (st["q"] * g if isinstance(g, int) else 0) + q) % 2
                pe.wait_ge(wh_ready, n + 1)
                moving(g, q)
                for t in range(4):
                    for k in range(4):
                        w = WH[slot][:, k, P * t:P * t + P]
                        o = pg[:, T * t:T * t + T]
                        first = q == 0 and k == 0 and t % 2 == 0
                        mm(o, w, hi[:, 4 * q + k, :], start=first, stop=False, skip_group_check=True)
                        mm(o, w, lo[:, 4 * q + k, :], start=False, stop=False, skip_group_check=True)
                pe.wait_ge(wl_ready, n + 1)
                pe.wait_ge(wlp_ready, n + 1)
                for t in range(4):
                    for k in range(4):
                        ins = mm(pg[:, T * t:T * t + T], WL[slot][:, k, P * t:P * t + P], hi[:, 4 * q + k, :],
                                 start=False, stop=(q == st["q"] - 1 and k == 3), skip_group_check=True)
                ins.then_inc(panel_used, 1)

        def square_sums_all(n):
            if n:
                pe.wait_ge(rt_ready, n)
            for q in range(4):
                pe.wait_ge(squared, 4 * n + q + 1)
                for k in range(4):
                    ins = mm(PS[:, 0:T], ONES[:, :], SQ[q % 2][:, k, :], start=(q == 0 and k == 0),
                             stop=(q == 3 and k == 3))
                ins.then_inc(sq_used, 1)

        pe.wait_ge(cst_full, 16)
        pe.wait_ge(par_full, 16 * 14)
        for b in range(5):
            r = P if b < 4 else 80
            ins = pe.transpose(PG[0][:, P * b:P * b + r], PROW[0:r, b, :], cst("ident")[0:r, 0:r])
        ins.then_inc(par_turned, 1)
        pe.wait_ge(ones_set, 3)
        reduce_unit(0)
        pe.wait_ge(x_full, 16)
        for g in range(4):
            if g == 0:
                pe.wait_ge(par_copied, 1)
            elif g >= 2:
                pe.wait_ge(x_copied, g - 1)
            for j in range(4):
                for h in range(2):
                    ins = pe.transpose(PG[g % 2][:, T * j + P * h:T * j + P * h + P],
                                       XIN[:, h, P * (4 * g + j):P * (4 * g + j) + P], cst("ident"))
            ins.then_inc(x_turned, 1)
        square_sums_all(0)
        for u in range(1, 4):
            reduce_unit(u)
        def lora_first(n, w, width, outs):
            for k in range(KT):
                pe.wait_ge(mix_ready, KT * n + k + 1)
                for j, o in enumerate(outs):
                    ins = mm(o, w(k, j), MIX[:, k, :], start=(k == 0 and j == 0), stop=(k == KT - 1),
                             skip_group_check=True)
                ins.then_inc(mix_used, 1)

        flat = lambda n: RAW[n][:, :, :].rearrange("p a b -> p (a b)")
        pe.wait_ge(lora_full[0], 16)
        lora_first(0, lambda k, j: flat(0)[:, LORA * k:LORA * k + LORA], LORA, [PT0[0:LORA, 0:T]])
        pe.wait_ge(lora_full[1], 16)
        lora_first(1, lambda k, j: flat(1)[:, LORA * k:LORA * k + LORA], LORA, [PT1[0:LORA, 0:T]])
        done = [0]

        def lora_second(mid, full, make):
            pe.wait_ge(lora_mid, mid)
            for w, v in full:
                pe.wait_ge(w, v)
            for g in range(4):
                gi = done[0]
                if gi >= 2:
                    pe.wait_ge(st_ready, gi - 1)
                for t in range(4):
                    ins = make(PG[gi % 2][:, T * t:T * t + T], 4 * g + t, t % 2 == 0)
                ins.then_inc(lora_done, 1)
                done[0] += 1

        lora_second(1, [(lora_full[0], 32)],
                    lambda o, j, first: mm(o, flat(0)[0:LORA, P * j:P * j + P], TW[:, :], start=first, stop=True,
                                           skip_group_check=True))
        pe.wait_ge(lora_full[2], 16)
        pe.wait_ge(lora_full[3], 16)
        g1 = [RAW[2 + n][:, :, :].rearrange("p a (b n) -> p (a b) n", b=2) for n in range(2)]
        lora_first(2, lambda k, j: g1[k // 8][:, k % 8, P * j:P * j + P], 0, [PT0[:, 0:T], PT0[:, T:2 * T]])
        lora_second(2, [(lora_full[1], 32)],
                    lambda o, j, first: mm(o, flat(1)[0:LORA, P * j:P * j + P], AW[:, :], start=first, stop=True,
                                           skip_group_check=True))

        def gate_second(o, j, first):
            mm(o, flat(2)[:, P * j:P * j + P], GW[:, 0, :], start=first, stop=False, skip_group_check=True)
            return mm(o, flat(3)[:, P * j:P * j + P], GW[:, 1, :], start=False, stop=True, skip_group_check=True)

        lora_second(3, [(lora_full[2], 32), (lora_full[3], 32)], gate_second)

        for s, name in enumerate(("r", "k", "v")):
            def moving(g, q, s=s):
                pe.wait_ge(mh_ready, 4 * s + q + 1)
                pe.wait_ge(ml_ready, 4 * s + q + 1)
            st = stages[name]
            with pe.Fori(0, 2) as i:
                for j in range(2):
                    pe.wait_ge(st_ready, 12 + 4 * s + 2 * i + j - 1)
                    group(st, 2 * i + j, MH, ML, j, moving)

        sid = cst("stacked_ident")
        pe.wait_ge(st_ready, 24)

        def scan_body(n, k):
            par, nxt = k % 2, (k + 1) % 2
            prep, inverse, recur, norm = k + 2 < KT, 0 <= k + 1 < KT, 0 <= k < KT, 0 <= k - 1 < KT

            heads = [slice(0, 64), slice(64, P)]

            def rhs(c):
                if recur:
                    if c == 0:
                        pe.wait_ge(tok_ready, n + 1)
                        pe.wait_ge(coef_ready, n + 1)
                        pe.wait_ge(ni_ready, n + 1)
                        if k >= 1:
                            pe.wait_ge(u_ready, 4 * n)
                    else:
                        pe.wait_ge(s_ready, 3 * n + c)
                    take_wait(PT0[:, 384:512])
                    for h in heads:
                        ins = mm(PT0[h, 0:C], AAK[par][h, c, :], TOKV[par][h, c, :], start=True, stop=(c == 0))
                        if c:
                            ins = mm(PT0[h, 0:C], AR[par][h, c, 0, :], SS[c % 2][h, :], start=False, stop=True)
                    ins.then_inc(rhs_done, 1)

            def solve(c):
                if recur:
                    pe.wait_ge(rhs_ready, 4 * n + c + 1)
                    take_wait(PT0[:, 384:512])
                    for h in heads:
                        ins = mm(PT0[h, C:2 * C], NI[par][h, c, :], RH[h, :], start=True, stop=True)
                    ins.then_inc(u_done, 1)

            def state(c):
                if not recur:
                    return
                pe.wait_ge(u_ready, 4 * n + c + 1)
                if c < NC - 1:
                    take_wait(PT0[:, 384:512])
                    for h in heads:
                        mm(PT0[h, 2 * C:3 * C], TOKBK[par][h, 0, c, :], UU[h, :], start=True, stop=False)
                        ins = mm(PT0[h, 2 * C:3 * C], TOKBK[par][h, 1, c, :], TOKV[par][h, c, :], start=False, stop=True)
                    ins.then_inc(sd_done, 1)
                if c == 0 and k >= 1:
                    pe.wait_ge(yc_ready, n)
                take_wait(PT1[:, 384:512])
                if c == 0:
                    for _ in range(WARM_UP):
                        mm(PT1[:, 256:512], ONESB[:, :], WARMB[:, :], start=True, stop=True)
                for h in heads:
                    yo = PT1[h, C * c:C * c + C]
                    if c:
                        mm(yo, AR[par][h, c, 1, :], SS[c % 2][h, :], start=True, stop=False)
                    mm(yo, ARB[par][h, c, :], UU[h, :], start=(c == 0), stop=False)
                    ins = mm(yo, ARK[par][h, c, :], TOKV[par][h, c, :], start=False, stop=True)
                ins.then_inc(y_done, 1)

            def level_p(lv):
                if not inverse:
                    return
                for hb in range(2):
                    if lv == 0:
                        pe.wait_ge(*((tok_ready, n + 2) if hb else (tokv_ready, n + 2)))
                    pe.wait_ge(nt_ready, 9 * n + 9 + (1 if lv == 0 else 2 * lv + hb))
                    pe.wait_ge(am_ready, 5 * n + 5 + lv + 1)
                    take_wait(PG[1][:, 512 * hb + 384:512 * hb + 512])
                    for c in range(2):
                        for h in heads:
                            ins = mm(PG[1][h, 512 * hb + C * c:512 * hb + C * c + C], AM[lv % 2][h, 2 * hb + c, :],
                                     NT[h, 2 * hb + c, 0, :], start=True, stop=True)
                    ins.then_inc(p_done, 1)

            def level_d(lv):
                if not inverse:
                    return
                for hb in range(2):
                    pe.wait_ge(p_copied, 10 * n + 10 + 2 * lv + hb + 1)
                    take_wait(PG[1][:, 512 * hb + 384:512 * hb + 512])
                    for c in range(2):
                        cc = 2 * hb + c
                        o = 512 * hb + 2 * C + 2 * C * c
                        for h in heads:
                            ins = mm(PG[1][h, o:o + C], NT[h, cc, 1, :], PC[h, cc, :], start=True, stop=True)
                            if lv < 4:
                                ins = mm(PG[1][h, o + C:o + 2 * C], PC[h, cc, :], NT[h, cc, 1, :],
                                         start=True, stop=True)
                    ins.then_inc(d_done, 1)

            rhs(0)
            if inverse:
                pe.wait_ge(ar_ready, n + 2)
                pe.wait_ge(b_ready, n + 2)
                pe.wait_ge(kw_ready, n + 2)
                if k >= 0:
                    pe.wait_ge(coef_ready, n + 1)
                    pe.wait_ge(ni_ready, n + 1)
                take_wait(PG[0][:, 0:P])
                for c in range(NC):
                    for h in heads:
                        ins = mm(PG[0][h, P * c:P * c + P], BST[h, c, :], AR[nxt][h, c, :, :], start=True, stop=True)
                ins.then_inc(pb_done, 1)
                take_wait(PG[1][:, 0:P])
                for c in range(NC):
                    for h in heads:
                        mm(PG[1][h, C * c:C * c + C], AR[nxt][h, c, 0, :], BST[h, c, :], start=True, stop=True)
                        ins = mm(PG[1][h, T + C * c:T + C * c + C], IN[nxt][h, 2, C * c:C * c + C], sid[h, :],
                                 start=True, stop=True)
                ins.then_inc(ast_done, 1)
            solve(0)
            if inverse:
                take_wait(PG[1][:, 2 * T:2 * T + P])
                for c in range(NC):
                    for h in heads:
                        mm(PG[1][h, 2 * T + C * c:2 * T + C * c + C], BST[h, c, :], sid[h, :], start=True, stop=True)
                        ins = mm(PG[1][h, 3 * T + C * c:3 * T + C * c + C], KW[h, C * c:C * c + C], sid[h, :],
                                 start=True, stop=True)
                ins.then_inc(tok_done, 1)
            state(0)
            if inverse:
                take_wait(PG[0][:, 512:512 + P])
                for c in range(NC):
                    for h in heads:
                        ins = mm(PG[0][h, 512 + P * c:512 + P * c + P], KW[h, C * c:C * c + C], AR[nxt][h, c, :, :],
                                 start=True, stop=True)
                ins.then_inc(pk_done, 1)
            level_p(0)
            rhs(1)
            level_d(0)
            solve(1)
            level_p(1)
            state(1)
            level_d(1)
            rhs(2)
            if prep:
                pe.wait_ge(ksq_ready, n + 3)
                if k + 2 >= 1:
                    pe.wait_ge(bv_ready, n + 2)
                if k >= 2:
                    pe.wait_ge(yt_read, n - 1)
                mm(PS[:, 0:T], cst("head_ones"), KSQ[:, :], start=True, stop=True).then_inc(ss_done, 1)
            level_p(2)
            solve(2)
            level_d(2)
            state(2)
            level_p(3)
            rhs(3)
            level_d(3)
            solve(3)
            if prep:
                pe.wait_ge(rr_ready, n + 3)
                pe.wait_ge(nrm_ready, n + 3)
                mm(PS[:, T:2 * T], cst("head_ones"), RR[:, :], start=True, stop=True).then_inc(bonus_done, 1)
            level_p(4)
            if norm:
                pe.wait_ge(yn_ready, n)
                if not prep:
                    pe.wait_ge(yt_read, n - 1)
                    pe.wait_ge(bv_ready, KT)
                take_wait(PS[:, 0:P])
                for c in range(NC):
                    for h in heads:
                        ins = mm(PS[h, C * c:C * c + C], YN[h, c, :], sid[h, :], start=True, stop=True)
                ins.then_inc(yt_done, 1)
            state(3)
            level_d(4)

        for n in range(-2, 2):
            scan_body(n, n)
        reduce_unit(4)
        with pe.Fori(0, 6) as i:
            for tt in range(2):
                scan_body(2 * i + 2 + tt, 2 + tt)
            reduce_unit(i + 5)
        for n in range(14, 18):
            scan_body(n, n)
            if n == 15:
                reduce_unit(11)

        def output_stage(name, hi, lo, moving, free):
            st = stages[name]
            p = st["g0"] % 2
            if st["q"] == 4:
                with pe.Fori(0, 2) as i:
                    for j in range(2):
                        if name == "o":
                            pe.wait_ge(y_ready, 2 * i + 1 if j else i + 1)
                        else:
                            free(2 * i + j, j)
                        group(st, 2 * i + j, hi, lo, (p + j) % 2, moving)
                    if name in CARRY:
                        reduce_unit(i + CARRY[name])
            else:
                for g in range(4):
                    free(g, g)
                    group(st, g, hi, lo, (p + g) % 2, moving)

        def by_tile(base):
            def moving(g, q):
                pe.wait_ge(mh_ready, base + 4 * q + 4)
                pe.wait_ge(ml_ready, base + 4 * q + 4)
            return moving

        YB = [4, 20]

        def ffn(l):
            base = 28 if l == 0 else 92
            for part in range(3):
                st = stages[f"gu{l}{part}"]
                h0 = 22 * l + sum(x for x, _ in PARTS[:part])
                if part:
                    pe.wait_ge(y_ready, YB[l] + 4 * part + 1)
                with pe.Fori(0, st["groups"] // 2) as i:
                    for j in range(2):
                        g = 2 * i + j
                        pe.wait_ge(hid_ready, h0 + g + 1)
                        group(st, g, MH, ML, (st["g0"] + j) % 2, by_tile(base))
                    if st["name"] in CARRY:
                        reduce_unit(i + CARRY[st["name"]])

                def moving(g, q, h0=h0):
                    pe.wait_ge(hh_ready, h0 + 2 * q + 2)
                    pe.wait_ge(hl_ready, h0 + 2 * q + 4)

                n0 = YB[l] + 4 * part
                last = h0 + st["groups"]

                def free(g, j, n0=n0, last=last):
                    pe.wait_ge(hid_ready, last + (2 if j else 1))
                    if isinstance(g, int):
                        if g >= 2:
                            pe.wait_ge(y_ready, n0 + g)
                    else:
                        pe.wait_ge(y_ready, n0 + g)

                output_stage(f"down{l}{part}", HH, HL, moving, free)

        st = stages["o"]
        pe.wait_ge(ml_ready, 12 + KT)
        output_stage("o", MH, ML, by_tile(12), lambda g, j: None)
        square_sums_all(1)
        square_sums_all(2)
        ffn(0)
        square_sums_all(3)
        square_sums_all(4)
        st = stages["kv"]
        group(st, 0, MH, ML, st["g0"] % 2, by_tile(44))
        reduce_unit(23)

        pe.wait_ge(kv_copied, 2)
        st = stages["q"]
        with pe.Fori(0, 2) as i:
            for j in range(2):
                pe.wait_ge(q_copied, 2 * i + 1 if j else i + 1)
                group(st, 2 * i + j, MH, ML, (st["g0"] + j) % 2, by_tile(60))
            reduce_unit(i + CARRY["q"])
        pe.wait_ge(q_copied, 5)
        mm(PT0[:, :], cst("rope_swap"), KR[:, :, :], start=True, stop=True).then_inc(swap_done, 1)
        pe.wait_ge(roped, 1)
        for g in range(4):
            ins = mm(PG[0][:, T * g:T * g + T], cst(f"dup{g % 2}"), KX[:, g // 2, :], start=(g % 2 == 0), stop=True,
                     skip_group_check=True)
        ins.then_inc(kd_done, 1)
        for w in range(NC):
            lo, m = (0, 64) if w == 0 else (64 * (w - 1), P)
            for j in range(2):
                ins = pe.transpose(PG[1][0:m, T * w + P * j:T * w + P * j + P], VR2[:, j, lo:lo + m], cst("ident"))
        ins.then_inc(vw_done, 1)
        pe.wait_ge(kd_ready, 1)
        pe.wait_ge(vw_ready, 1)
        for g in range(4):
            with pe.Fori(0, 2) as i:
                for tt in range(2):
                    n = 2 * i + tt + 4 * g
                    pe.wait_ge(roped, n + 1)
                    mm(PTT[tt][:, 0:T], cst("rope_swap"), QR[:, bass.ds(n, 1), :], start=True, stop=True)\
                      .then_inc(swap_done, 1)
                    pe.wait_ge(roped, n + 2)
                    take_wait(PTT[tt][:, 0:1])
                    for w in range(NC):
                        lo = 64 * w - 64 if w else 0
                        for e in range(2):
                            h = slice(64 * e, 64 * e + 64)
                            if w == 0:
                                ins = mm(PTT[tt][h, 64:P], QS[tt][h, 0:64], KD[h, g, 0:64], start=True, stop=True)
                            else:
                                ins = mm(PTT[tt][h, P * w:P * w + P], QS[tt][h, 64 * w:64 * w + 64],
                                         KD[h, g, lo:lo + P], start=True, stop=True)
                    ins.then_inc(sco_done, 1)
                    pe.wait_ge(norm_ready, n + 1)
                    for w in (1, 2, 3, 0):
                        m = 64 if w == 0 else P
                        ins = pe.transpose(PG[tt][0:m, P * w:P * w + P], PR[tt][:, w, P - m:P], cst("ident"))
                    ins.then_inc(pt_done, 1)
                    pe.wait_ge(pt_ready, n + 1)
                    for w in (1, 2, 3, 0):
                        m = 64 if w == 0 else P
                        for e in range(2):
                            ins = mm(PG[tt][64 * e:64 * e + 64, 512 + C * w:512 + C * w + C], VW[0:m, w, C * g:C * g + C],
                                     PT[tt][0:m, w, C * e:C * e + C], start=True, stop=True)
                    ins.then_inc(o_done, 1)
        pe.wait_ge(ml_ready, 92)
        output_stage("ao", MH, ML, by_tile(76), lambda g, j: pe.wait_ge(y_ready, 16 + g))
        square_sums_all(5)
        square_sums_all(6)
        ffn(1)
        square_sums_all(7)
        pe.wait_ge(x_ready, 16)
        for g in range(8):
            if g >= 2:
                pe.wait_ge(drained, g - 1)
            for j in range(4):
                k = 4 * (g % 4) + j
                ins = pe.transpose(PTT[g % 2][:, P * j:P * j + P], X[:, k, P * (g // 4):P * (g // 4) + P], cst("ident"))
            ins.then_inc(turned, 1)

    @block.vector
    def _(dve):
        step = Tally(v_step)

        def link(ins):
            dve.wait_ge(v_step, step.add(ins))

        def residue(n, slot=None):
            if isinstance(n, int):
                slot = n % 4
            dve.wait_ge(wh_ready, n + 1)
            if not (isinstance(n, int) and n < 2):
                dve.wait_ge(panel_used, n - 1)
            dve.tensor_tensor(WL[slot % 2][:, 0:2, :], RAW[slot][:, 0:2, :], WH[slot % 2][:, 0:2, :].bitcast(F32),
                              ALU.subtract).then_inc(wl_ready, 1)

        def ada_step(u, s):
            m = 16 * u + s
            dve.wait_ge(ada_full[s % 4], 16 * (4 * u + s // 4) + 16)
            if s == 0:
                if not (isinstance(u, int) and u == 0):
                    dve.wait_ge(red_done, u)
                dve.tensor_scalar(ACC[:, :], ADA[0][:, :], CA[:, 0:1], None, ALU.mult).then_inc(ada_used, 1)
            else:
                dve.wait_ge(ada_used, m)
                ins = dve.scalar_tensor_tensor(out=ACC[:, :], in0=ADA[s % 4][:, :], scalar=CA[:, s:s + 1],
                                               in1=ACC[:, :], op0=ALU.mult, op1=ALU.add)
                ins.then_inc(ada_used, 1)

        def ada_finish(u):
            dve.wait_ge(red_done, u + 1)
            dve.tensor_tensor(MODS[:, bass.ds(8 * u, 8)], PA[:, 0:8], PM[:, bass.ds(col["bias"] + 8 * u, 8)], ALU.add)\
               .then_inc(mods_ready, 1)

        def inverse_rms(n):
            dve.wait_ge(rt_ready, n + 1)
            dve.reciprocal(RS[:, :], RT[:, :]).then_inc(rs_ready, 1)
            dve.wait_ge(rs_ready, n + 1)

        def gains(scale, g, units):
            dve.wait_ge(mods_ready, units)
            link(dve.scalar_tensor_tensor(out=SV[:, :], in0=mod(scale), scalar=1.0, in1=pm(g), op0=ALU.add, op1=ALU.mult))

        def residual(n, gate, g, nx, units):
            dve.wait_ge(mods_ready, units)
            link(dve.tensor_tensor(GG[:, :], mod(gate), pm(g), ALU.mult))
            inverse_rms(n)
            for q in range(4):
                for k in range(4 * q, 4 * q + 4):
                    ins = dve.scalar_tensor_tensor(out=Y[:, k, :], in0=Y[:, k, :], scalar=GG[:, k:k + 1],
                                                   in1=RS[:, :], op0=ALU.mult, op1=ALU.mult)
                link(ins)
                dve.tensor_tensor(X[:, 4 * q:4 * q + 4, :], X[:, 4 * q:4 * q + 4, :], Y[:, 4 * q:4 * q + 4, :], ALU.add)\
                   .then_inc(x_ready, 1)
            dve.wait_ge(x_ready, nx + 4)

        def modulated(nh, nm, shift):
            for k in range(KT):
                dve.scalar_tensor_tensor(out=Y[:, k, :], in0=X[:, k, :], scalar=SV[:, k:k + 1], in1=RS[:, :],
                                         op0=ALU.mult, op1=ALU.mult).then_inc(scaled, 1)
                if k:
                    low(nm, k - 1, shift)
            low(nm, KT - 1, shift)

        def low(nm, k, shift):
            dve.wait_ge(mh_ready, nm + k + 1)
            dve.scalar_tensor_tensor(out=ML[:, k, :], in0=Y[:, k, :], scalar=mod(shift)[:, k:k + 1],
                                     in1=MH[:, k, :].bitcast(F32), op0=ALU.add, op1=ALU.subtract).then_inc(ml_ready, 1)

        dve.memset(GG[:, 0:1], 0.0).then_inc(hid_ready, 1)
        dve.memset(GG[:, 1:2], 0.0).then_inc(hid_ready, 1)
        dve.memset(GG[:, 2:3], 0.0).then_inc(hl_ready, 1)
        dve.memset(GG[:, 3:4], 0.0).then_inc(hl_ready, 1)
        dve.memset(GG[:, 4:5], 0.0).then_inc(y_ready, 1)
        dve.memset(GG[:, 5:6], 0.0).then_inc(q_copied, 1)
        dve.wait_ge(par_copied, 1)
        link(dve.tensor_scalar(OMK[:, :], pm("k_a"), -1.0, 1.0, ALU.mult, ALU.add))
        dve.wait_ge(ca_ready, 1)
        for u in range(4):
            for s in range(16):
                ada_step(u, s)
            ada_finish(u)
        gains("sc_m0", "g00", 4)
        inverse_rms(0)
        dve.wait_ge(x_turned, 4)
        for k in range(KT):
            dve.scalar_tensor_tensor(out=MIX[:, k, :], in0=X[:, k, :], scalar=SV[:, k:k + 1], in1=RS[:, :],
                                     op0=ALU.mult, op1=ALU.mult).then_inc(scaled, 1)
        dve.wait_ge(h_ready, KT)
        dve.tensor_tensor(XX[:, :, 1:T], H[:, :, 0:T - 1], H[:, :, 1:T], ALU.subtract)
        link(dve.tensor_scalar(XX[:, :, 0:1], H[:, :, 0:1], -1.0, None, ALU.mult))
        for n, i in enumerate((1, 4, 5)):
            for k in range(KT):
                if n:
                    dve.wait_ge(mix_used, KT * (n - 1) + k + 1)
                dve.scalar_tensor_tensor(out=MIX[:, k, :], in0=XX[:, k, :], scalar=pm(f"mu{i}")[:, k:k + 1],
                                         in1=H[:, k, :], op0=ALU.mult, op1=ALU.add).then_inc(mix_ready, 1)

        def mixture(nm):
            q, s = nm % 4, nm // 4
            if s == 0:
                dve.wait_ge(mix_used, 2 * KT + 4 * q + 4)
            else:
                dve.wait_ge(ml_ready, nm - 3)
            for k in range(4 * q, 4 * q + 4):
                ins = dve.scalar_tensor_tensor(out=MIX[:, k, :], in0=XX[:, k, :],
                                               scalar=pm(f"mu{(0, 2, 3)[s]}")[:, k:k + 1], in1=H[:, k, :],
                                               op0=ALU.mult, op1=ALU.add)
            ins.then_inc(mix_full, 1)
            dve.wait_ge(mh_ready, nm + 1)
            dve.tensor_tensor(ML[:, 4 * q:4 * q + 4, :], MIX[:, 4 * q:4 * q + 4, :],
                              MH[:, 4 * q:4 * q + 4, :].bitcast(F32), ALU.subtract).then_inc(ml_ready, 1)

        residue(0)
        for q in range(4):
            mixture(q)
        for s, name in enumerate(("r", "k", "v")):
            st = stages[name]
            for g in range(4):
                for q in range(4):
                    if st["p0"] + 4 * g + q + 1 < 48:
                        residue(st["p0"] + 4 * g + q + 1)
                    if g == 3 and q >= 1 and s < 2:
                        mixture(4 * (s + 1) + q - 1)
            if s < 2:
                mixture(4 * (s + 1) + 3)

        dve.wait_ge(g_full, 16)
        for stores in scr_stored:
            dve.wait_ge(stores, 16 * 12)
        bc = lambda x, *shape: x.to_broadcast([P, *shape])
        c4 = lambda x: x.rearrange("p (c t) -> p c t", c=NC)
        mask = lambda name: cst(name).unsqueeze(1)
        one = lambda x: x.rearrange("p (a t) -> p a t", a=1)
        pb = PG[0][:, 0:512].rearrange("p (c x t) -> p c x t", c=NC, x=2)
        pk = PG[0][:, 512:1024].rearrange("p (c x t) -> p c x t", c=NC, x=2)
        py = c4(PT1[:, 0:T])

        def scan_body(n, k, unit, prep_round=None):
            par, nxt = k % 2, (k + 1) % 2
            prep, inverse, recur, norm = k + 2 < KT, 0 <= k + 1 < KT, 0 <= k < KT, 0 <= k - 1 < KT
            r, key, v, aa, sw = (IN[par][:, x, :] for x in range(5))
            at_tile = lambda name, off: PM[:, bass.ds(col[name] + n + off, 1)]
            steps = iter(range(8 * par, 8 * par + 8))

            def carry(count):
                if recur:
                    for _ in range(count):
                        ada_step(unit, next(steps))

            def level_sum(lv):
                if not inverse:
                    return
                for hb in range(2):
                    dve.wait_ge(d_done, 10 * n + 10 + 2 * lv + hb + 1)
                    cs = slice(2 * hb, 2 * hb + 2)
                    pd = PG[1][:, 512 * hb + 2 * C:512 * hb + 6 * C].rearrange("p (c x t) -> p c x t", c=2, x=2)
                    if lv < 4:
                        dve.tensor_tensor(NT[:, cs, :, :], NT[:, cs, :, :], pd, ALU.add).then_inc(nt_ready, 1)
                    else:
                        ins = dve.tensor_tensor(NI[nxt][:, cs, :], pd[:, :, 0, :], NT[:, cs, 0, :], ALU.add)
                        if hb == 1:
                            ins.then_inc(ni_ready, 1)

            def decayed(c):
                if not recur:
                    return
                wc = WCA[:, bass.ds(n, 1), c:c + 1].rearrange("p a b -> p (a b)")
                if c:
                    link(dve.tensor_scalar(SW[:, :], SS[c % 2][:, :], wc, None, ALU.mult))
                    dve.wait_ge(sd_done, 3 * n + c + 1)
                    dve.scalar_tensor_tensor(out=SS[(c + 1) % 2][:, :], in0=PT0[:, 2 * C:3 * C], scalar=wc,
                                             in1=SW[:, :], op0=ALU.mult, op1=ALU.add).then_inc(s_ready, 1)
                else:
                    dve.wait_ge(sd_done, 3 * n + 1)
                    dve.tensor_scalar(SS[1][:, :], PT0[:, 2 * C:3 * C], wc, None, ALU.mult).then_inc(s_ready, 1)
                dve.wait_ge(s_ready, 3 * n + c + 1)

            if norm:
                dve.wait_ge(y_done, 4 * n)
                link(dve.tensor_reduce(MS[:, :], py, AX.X, ALU.add))
                link(dve.tensor_scalar(MS[:, :], MS[:, :], 1.0 / C, None, ALU.mult))
                if k >= 2:
                    dve.wait_ge(yn_ready, n - 1)
                dve.tensor_tensor(YC[:, :, :], py, bc(MS[:, :].unsqueeze(2), NC, C), ALU.subtract).then_inc(yc_ready, 1)
            if inverse:
                dve.wait_ge(pb_done, n + 2)
                dve.tensor_tensor(NT[:, :, 0, :], pb[:, :, 0, :], bc(mask("upper1"), NC, C), ALU.mult)
                dve.wait_ge(ast_ready, n + 2)
                link(dve.tensor_tensor(NT[:, :, 1, :], AST[:, :, :], bc(mask("lower1"), NC, C), ALU.mult))
                dve.tensor_tensor(NT[:, :, :, :], NT[:, :, :, :],
                                  cst("stacked_ident").unsqueeze(1).unsqueeze(1).to_broadcast([P, NC, 2, C]), ALU.add)\
                   .then_inc(nt_ready, 1)
                dve.wait_ge(nt_ready, 9 * n + 10)
            decayed(0)
            if prep:
                dve.wait_ge(in_full[par], 16 * ((n + 2) // 2 if isinstance(n, int) else prep_round) + 16)
                if k + 2 >= 1:
                    dve.wait_ge(exp_ready, n + 2)
                dve.tensor_tensor_scan(CUM[:, :], cst("carry"), sw, 0.0, ALU.mult, ALU.add).then_inc(cum_ready, 1)
                dve.tensor_scalar(T1[:, :], aa, at_tile("k_a", 2), OMK[:, bass.ds(n + 2, 1)], ALU.mult, ALU.add)\
                   .then_inc(t1_ready, 1)
            if inverse:
                dve.tensor_tensor(ARB[nxt][:, :, :], pb[:, :, 1, :], bc(mask("incl"), NC, C), ALU.mult)
            if 0 <= k - 2 < KT:
                low_part = lambda j: ML[:, bass.ds(j, 1), :]
                dve.wait_ge(mh_ready, 12 + n - 1)
                dve.tensor_tensor(low_part(n - 2), one(Y2[:, :]), MH[:, bass.ds(n - 2, 1), :].bitcast(F32), ALU.subtract)\
                   .then_inc(ml_ready, 1)
                dve.wait_ge(ml_ready, 12 + n - 1)
            carry(1)
            level_sum(0)
            if inverse:
                dve.wait_ge(pk_done, n + 2)
                dve.tensor_tensor(AAK[nxt][:, :, :], pk[:, :, 0, :], bc(mask("strict"), NC, C), ALU.mult)
                dve.tensor_tensor(ARK[nxt][:, :, :], pk[:, :, 1, :], bc(mask("incl"), NC, C), ALU.mult)\
                   .then_inc(coef_ready, 1)
            decayed(1)
            level_sum(1)
            if prep:
                dve.wait_ge(kp_ready, n + 3)
                dve.scalar_tensor_tensor(out=RR[:, :], in0=r, scalar=at_tile("r_k", 2), in1=KP[:, :], op0=ALU.mult,
                                         op1=ALU.mult).then_inc(rr_ready, 1)
            if norm:
                dve.wait_ge(yq_ready, n)
                link(dve.tensor_reduce(MS[:, :], YQ[:, :, :], AX.X, ALU.add))
                dve.tensor_scalar(VS[:, :], MS[:, :], 1.0 / C, GN_EPS, ALU.mult, ALU.add).then_inc(vs_ready, 1)
            carry(2)
            level_sum(2)
            decayed(2)
            if norm:
                dve.wait_ge(vr_ready, n)
                if k >= 2:
                    dve.wait_ge(yt_done, n - 1)
                dve.tensor_tensor(YN[:, :, :], YC[:, :, :], bc(VR[:, :].unsqueeze(2), NC, C), ALU.mult)\
                   .then_inc(yn_ready, 1)
            if prep:
                dve.wait_ge(nrm_ready, n + 3)
                link(dve.tensor_scalar(NRM[:, :], NRM[:, :], 1e-12, None, ALU.max))
                link(dve.reciprocal(NRM[:, :], NRM[:, :]))
                dve.scalar_tensor_tensor(out=KK[:, :], in0=key, scalar=at_tile("k_k", 2), in1=NRM[:, :], op0=ALU.mult,
                                         op1=ALU.mult).then_inc(kk_ready, 1)
                dve.wait_ge(kk_ready, n + 3)
            carry(2)
            level_sum(3)
            if prep:
                dve.wait_ge(exp_ready, n + 3)
                dve.tensor_copy(WCA[:, bass.ds(n + 2, 1), :].rearrange("p a c -> p (a c)"), c4(WI[:, :])[:, :, C - 1])
                if inverse:
                    dve.wait_ge(pk_done, n + 2)
                dve.wait_ge(kka_ready, n + 3)
                dve.tensor_tensor(BST[:, :, :], c4(KKA[:, :]), c4(WV[:, :]), ALU.mult).then_inc(b_ready, 1)
            carry(1)
            level_sum(4)
            if prep:
                if recur:
                    dve.wait_ge(y_done, 4 * n + 4)
                dve.scalar_tensor_tensor(out=AR[par][:, :, 0, :], in0=c4(KK[:, :]), scalar=-1.0, in1=c4(WE[:, :]),
                                         op0=ALU.mult, op1=ALU.mult)
                dve.tensor_tensor(AR[par][:, :, 1, :], c4(r), c4(WI[:, :]), ALU.mult).then_inc(ar_ready, 1)
            if norm:
                dve.wait_ge(yt_done, n)
                dve.tensor_scalar(Y2[:, :], PS[:, 0:T], at_tile("gn_g", -1), at_tile("gn_b", -1), ALU.mult, ALU.add)\
                   .then_inc(yt_read, 1)
                dve.wait_ge(yt_read, n)
            if prep:
                dve.wait_ge(bonus_done, n + 3)
                dve.tensor_tensor(BV[:, bass.ds(n + 2, 1), :], one(PS[:, T:2 * T]), one(v), ALU.mult)\
                   .then_inc(bv_ready, 1)
            if norm:
                link(dve.tensor_tensor(one(Y2[:, :]), one(Y2[:, :]), BV[:, bass.ds(n - 1, 1), :], ALU.add))
                dve.tensor_tensor(one(Y2[:, :]), one(Y2[:, :]), GATE[:, bass.ds(n - 1, 1), :], ALU.mult)\
                   .then_inc(yo_ready, 1)
            carry(2)
            if recur and par:
                ada_finish(unit)

        for n in range(-2, 2):
            scan_body(n, n, 4)
        base_step = step.v
        with dve.Fori(0, 6) as i:
            for tt in range(2):
                step.v, step.k = base_step + i * (2 * SCAN_LINKS) + tt * SCAN_LINKS, 0
                scan_body(2 * i + 2 + tt, 2 + tt, i + 5, i + 2)
                assert step.k == SCAN_LINKS, step.k
        step.v = base_step + 12 * SCAN_LINKS
        for n in range(14, 18):
            scan_body(n, n, 11)
        residue(48)

        def produce(st, g, u=None, odd=False):
            for q in range(st["q"]):
                n = st["p0"] + st["q"] * g + q + 1
                if not isinstance(n, int):
                    residue(n, (st["p0"] + q + 1) % 4)
                elif n < PANELS:
                    residue(n)
                if u is not None:
                    per = 4 if st["name"] == "kv" else 2
                    for s in range(per):
                        ada_step(u, per * q + s + (8 if odd else 0))

        def carried(st, i):
            return i + CARRY[st["name"]] if st["name"] in CARRY else None

        def ffn(l):
            for part in range(3):
                st = stages[f"gu{l}{part}"]
                hall = 22 * l + sum(x for x, _ in PARTS[:part])
                with dve.Fori(0, st["groups"] // 2) as i:
                    for j in range(2):
                        g = 2 * i + j
                        produce(st, g, carried(st, i), j == 1)
                        dve.wait_ge(sg_ready, hall + g + 1)
                        dve.wait_ge(hl_ready, hall + g + 1)
                        dve.tensor_tensor(HID[j][:, :, :], SG[j][:, :, :], PG[(st["g0"] + j) % 2][:, 512:1024]
                                          .rearrange("p (j t) -> p j t", j=2), ALU.mult).then_inc(hid_ready, 1)
                        dve.wait_ge(hh_ready, hall + g + 1)
                        dve.tensor_tensor(HL[:, bass.ds(2 * g, 2), :], HID[j][:, :, :],
                                          HH[:, bass.ds(2 * g, 2), :].bitcast(F32), ALU.subtract).then_inc(hl_ready, 1)
                    if st["name"] in CARRY:
                        ada_finish(carried(st, i))
                st = stages[f"down{l}{part}"]
                for g in range(4):
                    produce(st, g)
                    if part:
                        dve.wait_ge(panel_used, st["p0"] + st["q"] * (g + 1))
                        y = Y[:, 4 * g:4 * g + 4, :]
                        dve.wait_ge(y_ready, (5 if l == 0 else 21) + 4 * part)
                        dve.tensor_tensor(y, y, PG[(st["g0"] + g) % 2][:, :].rearrange("p (j t) -> p j t", j=4),
                                          ALU.add).then_inc(y_ready, 1)

        for g in range(4):
            produce(stages["o"], g)
        residual(1, "g_m0", "g01", 0, 12)
        gains("sc_f0", "g02", 12)
        inverse_rms(2)
        modulated(16, 28, "sh_f0")
        ffn(0)
        residual(3, "g_f0", "g03", 4, 16)
        gains("sc_kv", "kvg", 16)
        inverse_rms(4)
        modulated(32, 44, "sh_kv")
        st = stages["kv"]
        produce(st, 0, 23)
        ada_finish(23)
        dve.wait_ge(ml_ready, 60)
        gains("sc_m1", "g10", 20)
        dve.wait_ge(panel_used, st["p0"] + 4)
        modulated(48, 60, "sh_m1")
        dve.wait_ge(att_full, 32)
        for e in range(2):
            h = slice(64 * e, 64 * e + 64)
            link(dve.tensor_copy(SNK[h, :], SNKA[h, :].rearrange("p (j e) -> p e j", e=2)[:, e, :]))
        link(dve.tensor_copy(TURN[:, :], POSI[:, :]))
        link(dve.tensor_scalar(ANG[:, :], TURN[:, :], cst("freq"), None, ALU.mult))
        link(dve.tensor_scalar(TURN[:, :], ANG[:, :], float(1 / (2 * np.pi)), None, ALU.mult))
        link(dve.tensor_scalar(TURN[:, :], TURN[:, :], MAGIC, None, ALU.add))
        link(dve.tensor_scalar(TURN[:, :], TURN[:, :], -MAGIC, None, ALU.add))
        link(dve.scalar_tensor_tensor(out=ANG[:, :], in0=TURN[:, :], scalar=-TWO_PI_HI, in1=ANG[:, :],
                                      op0=ALU.mult, op1=ALU.add))
        link(dve.scalar_tensor_tensor(out=ANG[:, :], in0=TURN[:, :], scalar=-TWO_PI_LO, in1=ANG[:, :],
                                      op0=ALU.mult, op1=ALU.add))
        dve.tensor_scalar(ANG[:, :], ANG[:, :], -3.1415925, 3.1415925, ALU.max, ALU.min).then_inc(rope_ready, 1)
        dve.wait_ge(sin_ready, 1)
        link(dve.tensor_scalar(SIN[:, :], SIN[:, :], cst("rope_sign"), None, ALU.mult))
        link(dve.tensor_tensor(COS[:, :], COS[:, :], COS[:, :], ALU.mult))
        link(dve.tensor_scalar(COS[:, :], COS[:, :], -2.0, 1.0, ALU.mult, ALU.add))
        st = stages["q"]
        for g in range(4):
            produce(st, g, CARRY["q"] + g // 2, g % 2 == 1)
            if g % 2:
                ada_finish(CARRY["q"] + g // 2)
        two = lambda x: x.unsqueeze(1).to_broadcast([P, 2, T])
        dve.wait_ge(kv_copied, 2)
        dve.wait_ge(swap_done, 1)
        link(dve.tensor_tensor(KX[:, :, :], PT0[:, :].rearrange("p (j t) -> p j t", j=2), two(SIN[:, :]), ALU.mult))
        link(dve.tensor_tensor(KR[:, :, :], KR[:, :, :], two(COS[:, :]), ALU.mult))
        dve.tensor_tensor(KX[:, :, :], KX[:, :, :], KR[:, :, :], ALU.add).then_inc(roped, 1)
        dve.wait_ge(q_copied, 5)
        base_step = step.v
        with dve.Fori(0, KT // 2) as i:
            step.v, step.k = base_step + i * (2 * ATT_LINKS), 0
            for tt in range(2):
                n = 2 * i + tt
                one = lambda x: x.rearrange("p (a t) -> p a t", a=1)
                dve.wait_ge(swap_done, n + 2)
                link(dve.tensor_tensor(QT[tt][:, :], PTT[tt][:, 0:T], SIN[:, :], ALU.mult))
                link(dve.tensor_tensor(one(QS[tt][:, :]), QR[:, bass.ds(n, 1), :], one(COS[:, :]), ALU.mult))
                dve.tensor_tensor(QS[tt][:, :], QS[tt][:, :], QT[tt][:, :], ALU.add).then_inc(roped, 1)
                dve.wait_ge(sco_done, n + 1)
                ps = PTT[tt][:, :].rearrange("p (w k) -> p w k", w=NC)
                snk = SNK[:, bass.ds(n, 1)]
                dve.tensor_reduce(MX[tt][:, 0:1], ps[:, 0:1, 64:P], AX.X, ALU.max)
                link(dve.tensor_reduce(MX[tt][:, 1:4], ps[:, 1:4, :], AX.X, ALU.max))
                link(dve.tensor_scalar(MX[tt][:, :], MX[tt][:, :], ATT_SCALE, snk, ALU.mult, ALU.max))
                dve.tensor_scalar(ES[tt][:, :], MX[tt][:, :], -1.0, snk, ALU.mult, ALU.add)
                dve.tensor_scalar(NM[tt][:, :], MX[tt][:, :], -1.0, None, ALU.mult).then_inc(max_ready, 1)
                dve.wait_ge(prob_ready, n + 1)
                link(dve.tensor_tensor(DEN[tt][:, :], SU[tt][:, :], ES[tt][:, :], ALU.add))
                link(dve.reciprocal(DEN[tt][:, :], DEN[tt][:, :]))
                dve.tensor_scalar(PR[tt][:, 0, 64:P], PR[tt][:, 0, 64:P], DEN[tt][:, 0:1], None, ALU.mult)
                dve.tensor_tensor(PR[tt][:, 1:4, :], PR[tt][:, 1:4, :],
                                  DEN[tt][:, 1:4].unsqueeze(2).to_broadcast([P, 3, P]), ALU.mult).then_inc(norm_ready, 1)
                dve.wait_ge(mh_ready, 76 + n + 1)
                dve.tensor_tensor(ML[:, bass.ds(n, 1), :], PG[tt][:, 512:768].rearrange("p (a t) -> p a t", a=1),
                                  MH[:, bass.ds(n, 1), :].bitcast(F32), ALU.subtract).then_inc(ml_ready, 1)
                dve.wait_ge(ml_ready, 76 + n + 1)
            assert step.k == 2 * ATT_LINKS, step.k
        step.v = base_step + (KT // 2) * 2 * ATT_LINKS
        st = stages["ao"]
        for g in range(4):
            produce(st, g, CARRY["ao"] + g // 2, g % 2 == 1)
            if g % 2:
                ada_finish(CARRY["ao"] + g // 2)
        residual(5, "g_m1", "g11", 8, 22)
        gains("sc_f1", "g12", 26)
        inverse_rms(6)
        modulated(64, 92, "sh_f1")
        ffn(1)
        residual(7, "g_f1", "g13", 12, 28)

    ctx.close()


_INS = ["x", "c", "positions", "ada_w", "ada_b", "norm_g", "rwkv_mu", "rwkv_w_r", "rwkv_w_k", "rwkv_w_v",
        "rwkv_w0", "rwkv_w1", "rwkv_w2", "rwkv_a0", "rwkv_a1", "rwkv_a2", "rwkv_g1", "rwkv_g2", "rwkv_k_k",
        "rwkv_k_a", "rwkv_r_k", "rwkv_gn_g", "rwkv_gn_b", "rwkv_w_o", "kv_ada_w", "kv_ada_b", "kv_norm_g", "w_kv",
        "attn_w_q", "attn_sinks", "attn_w_o", "ffn_w_gu", "ffn_w_down"]


def kernel(**inputs):
    from concourse import bacc
    from concourse.bass_utils import run_bass_kernel_spmd

    nc = bacc.Bacc("TRN2", target_bir_lowering=False, num_devices=1)
    consts, at = constants()
    arrays = {"cst": consts}
    for name in _INS:
        arrays[name] = np.ascontiguousarray(inputs[name])
    args = {name: nc.dram_tensor(name, x.shape, mybir.dt.from_np(x.dtype), kind="ExternalInput").ap()
            for name, x in arrays.items()}
    out = nc.dram_tensor("out", (1, T, D), F32, kind="ExternalOutput").ap()
    trunk(nc, args, at, out)
    r = run_bass_kernel_spmd(nc, [arrays], core_ids=[0])
    return r.results[0]["out"]
```
